# Optimizing a Trainium2 kernel written in Bass

```python
import jax, jax.numpy as jnp
from jax import lax
import numpy as np

D_MODEL = 2048
BATCH = 1
SEQ = 512
DEPTH = 1

CHUNK = 64
Q_BLOCK = 128
N_MIXERS = 3
N_HEADS = 4
HEAD_DIM = 256
ATTN_WIDTH = N_HEADS * HEAD_DIM
DIFF_QK_DIM = HEAD_DIM // 2
D_FF = -(-8 * D_MODEL // (3 * 256)) * 256
RMS_EPS = 1e-6
DIFF_EPS = 1e-5
ALIBI_MAX_EXP = 8.0
HI = lax.Precision.HIGHEST

kernel_name = "chunk_causal_hybrid_fox_stickbreak_diffattn"

def _rmsnorm(x, g, eps=RMS_EPS):
    xf = x.astype(jnp.float32)
    y = xf * lax.rsqrt(jnp.mean(xf * xf, axis=-1, keepdims=True) + eps)
    return (y * g.astype(jnp.float32)).astype(x.dtype)

def _heads(a):
    b, s, _ = a.shape
    return a.reshape(b, s, N_HEADS, -1).transpose(0, 2, 1, 3)

def _merge_heads(o):
    b, h, s, dv = o.shape
    return o.transpose(0, 2, 1, 3).reshape(b, s, h * dv)

def _positions(t0, L):
    t = t0 + jnp.arange(Q_BLOCK, dtype=jnp.int32)
    kpos = jnp.arange(L, dtype=jnp.int32)
    return t, kpos

def _forgetting_attention(h, w_in, b_f, w_out):
    b, s, _ = h.shape
    A = ATTN_WIDTH
    proj = h @ w_in
    q = _heads(proj[..., :A]) * (HEAD_DIM ** -0.5)
    k = _heads(proj[..., A:2 * A])
    v = _heads(proj[..., 2 * A:3 * A])
    f_logit = proj[..., 3 * A:].astype(jnp.float32) + b_f.astype(jnp.float32)
    cum = jnp.cumsum(jax.nn.log_sigmoid(f_logit), axis=1).transpose(0, 2, 1)
    outs = []
    for t0 in range(0, s, Q_BLOCK):
        L = t0 + Q_BLOCK
        t, kpos = _positions(t0, L)
        logits = (jnp.einsum('bhqd,bhkd->bhqk', q[:, :, t0:L], k[:, :, :L]).astype(jnp.float32)
                  + cum[:, :, t0:L, None] - cum[:, :, None, :L])
        mask = kpos[None, :] <= t[:, None]
        p = jax.nn.softmax(jnp.where(mask, logits, -jnp.inf), axis=-1)
        outs.append(jnp.einsum('bhqk,bhkd->bhqd', p.astype(v.dtype), v[:, :, :L]))
    return _merge_heads(jnp.concatenate(outs, axis=2)) @ w_out

def _stick_breaking_attention(h, w_in, w_out):
    b, s, _ = h.shape
    A = ATTN_WIDTH
    proj = h @ w_in
    q = _heads(proj[..., :A]) * (HEAD_DIM ** -0.5)
    k = _heads(proj[..., A:2 * A])
    v = _heads(proj[..., 2 * A:])
    upper = jnp.tril(jnp.ones((Q_BLOCK, Q_BLOCK), jnp.float32), -1)
    outs = []
    for t0 in range(0, s, Q_BLOCK):
        L = t0 + Q_BLOCK
        n = L // Q_BLOCK
        t, kpos = _positions(t0, L)
        z = jnp.einsum('bhqd,bhkd->bhqk', q[:, :, t0:L], k[:, :, :L]).astype(jnp.float32)
        mask = kpos[None, :] < t[:, None]
        lom = jnp.where(mask, jax.nn.log_sigmoid(-z), 0.0)
        lom5 = lom.reshape(b, N_HEADS, Q_BLOCK, n, Q_BLOCK)
        inner = jnp.einsum('bhqnk,kj->bhqnj', lom5, upper, precision=HI)
        later = jnp.tril(jnp.ones((n, n), jnp.float32), -1)
        cross = jnp.einsum('bhqm,mn->bhqn', lom5.sum(-1), later, precision=HI)
        tail = (inner + cross[..., None]).reshape(b, N_HEADS, Q_BLOCK, L)
        a = jnp.where(mask, jnp.exp(jax.nn.log_sigmoid(z) + tail), 0.0)
        outs.append(jnp.einsum('bhqk,bhkd->bhqd', a.astype(v.dtype), v[:, :, :L]))
    return _merge_heads(jnp.concatenate(outs, axis=2)) @ w_out

def _differential_attention(h, w_in, lq1, lk1, lq2, lk2, subln, w_out, lambda_init):
    b, s, _ = h.shape
    A = ATTN_WIDTH
    f32 = jnp.float32
    proj = h @ w_in
    q = proj[..., :A].reshape(b, s, N_HEADS, 2, DIFF_QK_DIM).transpose(3, 0, 2, 1, 4) * (DIFF_QK_DIM ** -0.5)
    k = proj[..., A:2 * A].reshape(b, s, N_HEADS, 2, DIFF_QK_DIM).transpose(3, 0, 2, 1, 4)
    v = _heads(proj[..., 2 * A:])
    lam = (jnp.exp(jnp.sum(lq1.astype(f32) * lk1.astype(f32)))
           - jnp.exp(jnp.sum(lq2.astype(f32) * lk2.astype(f32))) + lambda_init)
    slopes = jnp.exp2(-ALIBI_MAX_EXP * jnp.arange(1, N_HEADS + 1, dtype=f32) / N_HEADS)
    outs = []
    for t0 in range(0, s, Q_BLOCK):
        L = t0 + Q_BLOCK
        t, kpos = _positions(t0, L)
        dist = jnp.abs(t[:, None] - kpos[None, :]).astype(f32)
        bias = -slopes[:, None, None] * dist[None]
        mask = (kpos // CHUNK)[None, :] <= (t // CHUNK)[:, None]

        def probs(qq, kk):
            logits = jnp.einsum('bhqd,bhkd->bhqk', qq[:, :, t0:L], kk[:, :, :L]).astype(f32) + bias
            return jax.nn.softmax(jnp.where(mask, logits, -jnp.inf), axis=-1)

        a = probs(q[0], k[0]) - lam * probs(q[1], k[1])
        outs.append(jnp.einsum('bhqk,bhkd->bhqd', a.astype(v.dtype), v[:, :, :L]))
    o = _rmsnorm(jnp.concatenate(outs, axis=2), subln, DIFF_EPS) * (1.0 - lambda_init)
    return _merge_heads(o) @ w_out

def _swiglu(h, w_gate_up, w_down):
    gu = h @ w_gate_up
    g, u = gu[..., :D_FF], gu[..., D_FF:]
    return (jax.nn.silu(g) * u) @ w_down

def setup_inputs(seed: int = 0) -> dict:
    key = jax.random.key(seed)
    keys = jax.random.split(key, 20)
    D, H, A = D_MODEL, N_HEADS, ATTN_WIDTH
    n_fox = len(range(0, DEPTH, N_MIXERS))
    n_sb = len(range(1, DEPTH, N_MIXERS))
    n_diff = len(range(2, DEPTH, N_MIXERS))

    def nrm(i, shape, scale):
        return jax.random.normal(keys[i], shape, jnp.float32) * scale

    return {
        "x": nrm(0, (BATCH, SEQ, D), 1.0),
        "norm_mix": 1.0 + nrm(1, (DEPTH, D), 0.02),
        "fox_w_in": nrm(2, (n_fox, D, 3 * A + H), D ** -0.5),
        "fox_b_f": 2.0 + nrm(3, (n_fox, H), 0.5),
        "fox_w_out": nrm(4, (n_fox, A, D), A ** -0.5),
        "sb_w_in": nrm(5, (n_sb, D, 3 * A), D ** -0.5),
        "sb_w_out": nrm(6, (n_sb, A, D), A ** -0.5),
        "diff_w_in": nrm(7, (n_diff, D, 3 * A), D ** -0.5),
        "diff_lambda_q1": nrm(8, (n_diff, DIFF_QK_DIM), 0.1),
        "diff_lambda_k1": nrm(9, (n_diff, DIFF_QK_DIM), 0.1),
        "diff_lambda_q2": nrm(10, (n_diff, DIFF_QK_DIM), 0.1),
        "diff_lambda_k2": nrm(11, (n_diff, DIFF_QK_DIM), 0.1),
        "diff_subln": 1.0 + nrm(12, (n_diff, HEAD_DIM), 0.02),
        "diff_w_out": nrm(13, (n_diff, A, D), A ** -0.5),
        "norm_ffn": 1.0 + nrm(14, (DEPTH, D), 0.02),
        "ffn_w_gate_up": nrm(15, (DEPTH, D, 2 * D_FF), D ** -0.5),
        "ffn_w_down": nrm(16, (DEPTH, D_FF, D), D_FF ** -0.5),
        "final_norm": 1.0 + nrm(17, (D,), 0.02),
    }

def reference(x, norm_mix, fox_w_in, fox_b_f, fox_w_out, sb_w_in, sb_w_out,
              diff_w_in, diff_lambda_q1, diff_lambda_k1, diff_lambda_q2, diff_lambda_k2,
              diff_subln, diff_w_out, norm_ffn, ffn_w_gate_up, ffn_w_down, final_norm):
    for i in range(DEPTH):
        kind, j = i % N_MIXERS, i // N_MIXERS
        h = _rmsnorm(x, norm_mix[i])
        if kind == 0:
            y = _forgetting_attention(h, fox_w_in[j], fox_b_f[j], fox_w_out[j])
        elif kind == 1:
            y = _stick_breaking_attention(h, sb_w_in[j], sb_w_out[j])
        else:
            lambda_init = 0.8 - 0.6 * float(np.exp(-0.3 * i))
            y = _differential_attention(h, diff_w_in[j], diff_lambda_q1[j], diff_lambda_k1[j],
                                        diff_lambda_q2[j], diff_lambda_k2[j], diff_subln[j],
                                        diff_w_out[j], lambda_init)
        x = x + y
        h = _rmsnorm(x, norm_ffn[i])
        x = x + _swiglu(h, ffn_w_gate_up[i], ffn_w_down[i])
    return _rmsnorm(x, final_norm)


_drawn_inputs = setup_inputs


def setup_inputs(seed=0):
    import zlib

    import numpy as np

    out = dict(_drawn_inputs(seed))
    spreads = {}
    factors = {'norm_mix': 4.331, 'norm_ffn': 4.0, 'final_norm': 2.822}
    for name, (base, spread) in spreads.items():
        noise = np.random.default_rng([zlib.crc32(name.encode()), seed]).standard_normal(out[name].shape)
        drawn = base * np.exp(spread * noise) if base else spread * noise
        out[name] = __import__('jax').numpy.asarray(drawn.astype(out[name].dtype))
    for name, factor in factors.items():
        out[name] = (out[name] * factor).astype(out[name].dtype)
    return out
```

```python
from contextlib import ExitStack

import concourse.bass as bass
from concourse import mybir

F32 = mybir.dt.float32
F32R = mybir.dt.float32r
ALU = mybir.AluOpType
ACT = mybir.ActivationFunctionType
AX = mybir.AxisListType.X

P = 128
SLAB = 2048
RAW = 3
RING = 2
BANK = 512
RMS_EPS = 1e-6
FLT_MAX = 3.4028234e38
QK, VV = 4, 2
PER_HEAD = QK + VV
PASSES = ((0, 0), (0, 1), (1, 0))


class At:

    def __init__(self, off, per=0, i=0):
        assert per % (RAW * RING) == 0
        self.off, self.per, self.i = off, per, i
        self.raw, self.ring = off % RAW, off % RING

    def count(self, more=0):
        return self.per * self.i + (self.off + more)

    def landed(self):
        return (16 * (self.per // RAW)) * self.i + 16 * (self.off // RAW + 1)

    def plus(self, j):
        return At(self.off + j, self.per, self.i)


def fox_layer(nc, x, norm_mix, w_in, b_f, w_out, norm_ffn, w_gu, w_down, norm_out, out):
    _, S, D = x.shape
    H = b_f.shape[1]
    A = w_out.shape[1]
    HD = A // H
    F = w_down.shape[1]
    NT, ND = S // P, D // P
    NH = HD // P
    NK = A // P
    NC = D // BANK
    G = 4
    GROUPS = F // P // G
    FFN = 3 * G
    SCALE = HD ** -0.5
    FIRST_WO = PER_HEAD * H
    FIRST_FFN = FIRST_WO + 2 * NC
    SLABS = FIRST_FFN + FFN * GROUPS
    TRI = NT * (NT + 1) // 2 * P
    assert S == BANK and ND * P == SLAB and NC == NT == G == 4 and NH == 2 and GROUPS * G * P == F
    assert FIRST_FFN % RING == 0 and SCALE == 2.0 ** -4
    p_at = [tb * (tb + 1) // 2 * P for tb in range(NT)]
    pt_at = {0: (0, 0), 1: (1, 0), 3: (1, 3 * P), 2: (2, 0)}
    pt_cols = [BANK, BANK, 2 * P]
    PT_BANKS = len(pt_cols)

    x_v = x.rearrange("a (t p) d -> p (a t) d", p=P)
    out_v = out.rearrange("a (t p) d -> p (a t) d", p=P)
    w_in_v = w_in.rearrange("a (c p) n -> p (a c) n", p=P)
    w_out_v = w_out.rearrange("a (k p) n -> p (a k) n", p=P)
    w_gu_v = w_gu.rearrange("a (c p) n -> p (a c) n", p=P)
    w_down_v = w_down.rearrange("a (f p) n -> p (a f) n", p=P)

    with ExitStack() as ctx:
        def sb(name, shape, dt=F32):
            return ctx.enter_context(nc.sbuf_tensor(name, shape, dt))

        def sem(name):
            return ctx.enter_context(nc.semaphore(name))

        hT = [sb(f"hT_{n}", [P, ND, S], F32R) for n in ("hi", "lo")]
        split = [sb(f"split_{n}", [P, RING, SLAB], F32R) for n in ("hi", "lo")]
        raw = sb("raw", [P, RAW, SLAB])
        oT = [sb(f"oT_{n}", [P, NK, S], F32R) for n in ("hi", "lo")]
        tmp = sb("tmp", [P, 4, BANK])
        ident = sb("ident", [P, P])
        bound = sb("bound", [P, P])
        with nc.sbuf_tensor("xres", [P, NT, D], F32) as xres, nc.sbuf_tensor("gain", [P, D], F32) as gain:
            pass
        qk = [[sb(f"{w}T_{n}", [P, NH, S], F32R) for n in ("hi", "lo")] for w in "qk"]
        v = [sb(f"v_{n}", [P, NT, HD], F32R) for n in ("hi", "lo")]
        pT = [sb(f"pT_{n}", [P, TRI], F32R) for n in ("hi", "lo")]
        vT = sb("vT", [P, NH, S])
        decay_t = sb("decay_t", [P, S], F32R)
        decay_s = sb("decay_s", [P, S], F32R)
        decay_h = sb("decay_h", [P, S], F32R)
        rows = sb("rows", [P, H, 4])
        row_of = sb("row_of", [P, 8])
        head_of = sb("head_of", [P, H])
        wf = sb("wf", [P, ND, H])
        bf = sb("bf", [P, 1])
        half = sb("half", [P, 1])
        sumsq = sb("sumsq", [P, NT, NC])
        var = sb("var", [P, NT])
        rstd = sb("rstd", [P, NT])
        negmax = sb("negmax", [P, NT])
        rowsum = sb("rowsum", [P, NT])
        rinv = sb("rinv", [P, NT])

        ps = ctx.enter_context(nc.psum_tensor("ps", [P, 8, BANK], F32))
        PROJ = (0, 1)
        PVB = (2, 3)
        SC = (4, 5, 6, 7)
        YB = ((0, 1, 7, 4), (2, 3, 5, 6))
        TP = (SC, YB[0])

        x_in = [sem(f"x_in{i}") for i in range(NT)]
        gain_in = sem("gain_in")
        small_in = sem("small_in")
        raw_in = [sem(f"raw_in{i}") for i in range(RAW)]
        out_done = sem("out_done")
        hi_ready = sem("hi_ready")
        lo_ready = sem("lo_ready")
        slab_used = sem("slab_used")
        const_set = sem("const_set")
        sq_done = sem("sq_done")
        stat = sem("stat")
        var_ready = sem("var_ready")
        rstd_ready = sem("rstd_ready")
        h_ready = sem("h_ready")
        h_turned = sem("h_turned")
        hT_hi = sem("hT_hi")
        hT_done = sem("hT_done")
        pad_hi = sem("pad_hi")
        pad_lo = sem("pad_lo")
        f_done = sem("f_done")
        gate_v = sem("gate_v")
        gate_s = sem("gate_s")
        qk_hi = sem("qk_hi")
        qk_done = sem("qk_done")
        v_taken = sem("v_taken")
        decay_ready = sem("decay_ready")
        s_done = sem("s_done")
        masked = sem("masked")
        max_ready = sem("max_ready")
        exp_done = sem("exp_done")
        inv_ready = sem("inv_ready")
        p_ready = sem("p_ready")
        vt_done = sem("vt_done")
        v_hi = sem("v_hi")
        v_ready = sem("v_ready")
        pt_done = sem("pt_done")
        pt_hi = sem("pt_hi")
        pt_ready = sem("pt_ready")
        pv_done = sem("pv_done")
        o_hi = sem("o_hi")
        o_ready = sem("o_ready")
        y_done = sem("y_done")
        added = sem("added")
        silu_done = sem("silu_done")
        a_done = sem("a_done")
        a_hi = sem("a_hi")
        a_ready = sem("a_ready")
        normed = sem("normed")

        block = ctx.enter_context(nc.Block())

        def f32(ap):
            return ap.bitcast(F32)

        def tmp_row(tb):
            return tmp[:, :, :].rearrange("p a b -> p (a b)")[:, p_at[tb]:p_at[tb] + (tb + 1) * P]

        def pad(part):
            return oT[0][:, part * 4:(part + 1) * 4, :].rearrange("p a b -> p (a b)").rearrange(
                "p (k n) -> p k n", n=P)

        def wait_used(eng, at):
            n = at.off
            if n < FIRST_WO:
                eng.wait_ge(slab_used, at.per * at.i + (n + 1))
            elif n < FIRST_FFN:
                cb, second = divmod(n - FIRST_WO, 2)
                if second:
                    eng.wait_ge(y_done, NT * (cb + 1))
                else:
                    eng.wait_ge(slab_used, FIRST_WO + cb + 1)
            else:
                j = n - FIRST_FFN
                if j < 2 * G:
                    eng.wait_ge(slab_used, (2 * G) * at.i + (FIRST_WO + NC + j + 1))
                else:
                    eng.wait_ge(y_done, (NT * NC) * at.i + (NT * NC + NT * (j - 2 * G + 1)))

        def slab(parts, at, part, tile, cols):
            return parts[part][:, at.ring, tile * cols:(tile + 1) * cols]

        @block.sync
        def _(sp):
            def load(at, view, source, first=False):
                if not first:
                    sp.wait_ge(lo_ready, at.count(1 - RAW))
                sp.dma_start(view, source).then_inc(raw_in[at.raw], 16)

            def tile_of(at, cols):
                return raw[:, at.raw, :].rearrange("p (k n) -> p k n", n=cols)

            def load_head(h):
                at = At(0, PER_HEAD, h)
                for j in range(PER_HEAD):
                    a = at.plus(j)
                    col = h * HD + ((j // NH) * A + (j % NH) * P)
                    load(a, tile_of(a, P), w_in_v[:, :, bass.ds(col, P)],
                         first=isinstance(h, int) and j < RAW)

            for tb in range(NT):
                sp.dma_start(xres[:, tb, :], x_v[:, tb, :]).then_inc(x_in[tb], 16)
            load_head(0)
            with sp.Fori(1, H) as h:
                load_head(h)
            for j in range(2 * NC):
                a = At(FIRST_WO + j)
                cb, kt = j // 2, (j % 2) * (NK // 2)
                load(a, tile_of(a, BANK), w_out_v[:, kt:kt + NK // 2, cb * BANK:(cb + 1) * BANK])
            with sp.Fori(0, GROUPS) as g:
                at = At(FIRST_FFN, FFN, g)
                for j in range(2 * G):
                    a = at.plus(j)
                    load(a, tile_of(a, P), w_gu_v[:, :, bass.ds(g * (G * P) + ((j // 2) * P + (j % 2) * F), P)])
                for cb in range(NC):
                    a = at.plus(2 * G + cb)
                    load(a, tile_of(a, BANK), w_down_v[:, bass.ds(g * G, G), cb * BANK:(cb + 1) * BANK])
            for n in range(2 * NT):
                tb, c = n // 2, (n % 2) * (D // 2)
                sp.wait_ge(normed, n + 1)
                sp.dma_start(out_v[:, tb, c:c + D // 2], xres[:, tb, c:c + D // 2]).then_inc(out_done, 16)
            sp.wait_ge(out_done, 16 * 2 * NT)

        @block.gpsimd
        def _(pool):
            nc.gpsimd.memset(half[:], -0.5).then_inc(const_set, 1)
            nc.gpsimd.memset(bf[:], 0.0).then_inc(const_set, 1)
            nc.gpsimd.memset(ident[:], 0.0).then_inc(const_set, 1)
            nc.gpsimd.memset(bound[:], FLT_MAX).then_inc(const_set, 1)
            nc.gpsimd.memset(rows[:], 0.0).then_inc(const_set, 1)
            pool.wait_ge(const_set, 5)
            nc.gpsimd.affine_select(out=ident[:], in_=ident[:], compare_op=ALU.not_equal, fill=1.0, base=0,
                                    pattern=[[-1, P]], channel_multiplier=1).then_inc(const_set, 1)
            for part in range(2):
                nc.gpsimd.memset(oT[0][:, part * 4:(part + 1) * 4, :].bitcast(F32), 0.0).then_inc(const_set, 1)
            nc.gpsimd.affine_select(out=bound[:], in_=bound[:], compare_op=ALU.is_ge, fill=-FLT_MAX, base=0,
                                    pattern=[[-1, P]], channel_multiplier=1).then_inc(const_set, 1)
            nc.gpsimd.affine_select(out=rows[:], in_=rows[:], compare_op=ALU.not_equal, fill=1.0, base=0,
                                    pattern=[[-32, H], [-1, 4]], channel_multiplier=1).then_inc(const_set, 1)
            for n in range(3 * NT):
                t = n % NT
                pool.wait_ge(var_ready, n + 1)
                nc.gpsimd.tensor_tensor(out=rstd[:, t:t + 1], in0=var[:, t:t + 1], in1=half[:],
                                        op=ALU.pow).then_inc(rstd_ready, 1)

        CONSTS = 10

        @block.scalar
        def _(act):
            def split_hi(at, first=False):
                act.wait_ge(raw_in[at.raw], at.landed())
                if not first:
                    wait_used(act, at.plus(-RING))
                nc.scalar.activation(split[0][:, at.ring, :], raw[:, at.raw, :], ACT.Copy).then_inc(hi_ready, 1)

            def take_hT(norm, tb):
                for q in range(4):
                    act.wait_ge(h_turned, 4 * NT * norm + 4 * tb + q + 1)
                    nc.scalar.activation(hT[0][:, 4 * q:4 * q + 4, tb * P:(tb + 1) * P],
                                         ps[:, TP[norm][q], :].rearrange("p (c t) -> p c t", t=P),
                                         ACT.Copy).then_inc(hT_hi, 1)

            def softmax(h):
                for tb in range(NT):
                    act.wait_ge(max_ready, NT * h + (tb + 1))
                    nc.scalar.activation(tmp_row(tb), ps[:, SC[tb], 0:(tb + 1) * P], ACT.Exp,
                                         bias=negmax[:, tb:tb + 1],
                                         accum_out=rowsum[:, tb:tb + 1]).then_inc(exp_done, 1)

            def take_v(h):
                for b in range(2):
                    act.wait_ge(vt_done, 2 * h + (b + 1))
                    nc.scalar.activation(v[0][:, 2 * b:2 * b + 2, :],
                                         ps[:, PVB[b], :].rearrange("p (t d) -> p t d", d=HD),
                                         ACT.Copy).then_inc(v_hi, 1)

            def take_pT(h):
                for b in range(PT_BANKS):
                    act.wait_ge(pt_done, PT_BANKS * h + (b + 1))
                    nc.scalar.activation(pT[0][:, b * BANK:b * BANK + pt_cols[b]], ps[:, SC[b], 0:pt_cols[b]],
                                         ACT.Copy).then_inc(pt_hi, 1)

            def take_o(h):
                for d in range(NH):
                    act.wait_ge(pv_done, NH * h + (d + 1))
                    nc.scalar.activation(oT[0][:, h * NH + d, :], ps[:, PVB[d], :], ACT.Copy).then_inc(o_hi, 1)

            def take_qk(h, at, j):
                wait_used(act, at.plus(j))
                nc.scalar.activation(qk[j // NH][0][:, j % NH, :], ps[:, PROJ[j % 2], :], ACT.Copy,
                                     scale=SCALE if j < NH else 1.0).then_inc(qk_hi, 1)

            def head(at, h, before=None):
                fresh = before is None
                split_hi(at.plus(1), first=fresh)
                if not fresh:
                    softmax(before)
                take_qk(h, at, 0)
                split_hi(at.plus(2))
                if not fresh:
                    take_v(before)
                take_qk(h, at, 1)
                split_hi(at.plus(3))
                if not fresh:
                    take_pT(before)
                take_qk(h, at, 2)
                split_hi(at.plus(4))
                if not fresh:
                    take_o(before)
                take_qk(h, at, 3)
                split_hi(at.plus(5))
                for j in range(VV):
                    wait_used(act, at.plus(QK + j))
                    nc.scalar.activation(vT[:, j, :], ps[:, PROJ[j % 2], :], ACT.Copy).then_inc(v_taken, 1)
                    if j == 0:
                        split_hi(at.plus(6))

            act.dma_start(gain[:], norm_mix.rearrange("a d -> (a d)").partition_broadcast(P)).then_inc(gain_in, 16)
            act.wait_ge(const_set, 5)
            with nc.allow_non_contiguous_dma(reason="the gate's four columns"):
                act.dma_start(wf[:], w_in_v[:, :, 3 * A:3 * A + H]).then_inc(small_in, 16)
            for h in range(H):
                for r in range(4):
                    act.dma_start(bf[32 * h + r:32 * h + r + 1, :], b_f[0:1, h:h + 1]).then_inc(small_in, 16)
            SMALLS = 16 * (1 + 4 * H)
            for tb in range(NT):
                act.wait_ge(x_in[tb], 16)
                if tb:
                    act.wait_ge(sq_done, tb)
                nc.scalar.activation(ps[:, 0:4, :], xres[:, tb, :].rearrange("p (c n) -> p c n", n=BANK),
                                     ACT.Square, accum_out=sumsq[:, tb, 0:1]).then_inc(sq_done, 1)
                if tb:
                    take_hT(0, tb - 1)
            act.wait_ge(small_in, SMALLS)
            act.wait_ge(const_set, CONSTS)
            for r in range(4):
                nc.scalar.activation(pad(0)[:, :, r::32], wf[:], ACT.Copy).then_inc(pad_hi, 1)
            take_hT(0, NT - 1)
            split_hi(At(0), first=True)
            act.wait_ge(gate_v, 1)
            nc.scalar.activation(tmp[:, 1, :], tmp[:, 0, :], ACT.Abs).then_inc(gate_s, 1)
            act.wait_ge(gate_s, 1)
            nc.scalar.activation(tmp[:, 2, :], tmp[:, 1, :], ACT.Exp, scale=-1.0).then_inc(gate_s, 1)
            act.wait_ge(gate_s, 2)
            nc.scalar.activation(tmp[:, 3, :], tmp[:, 2, :], ACT.Ln, bias=1.0).then_inc(gate_s, 1)
            head(At(0, PER_HEAD, 0), 0)
            with act.Fori(1, H) as h:
                head(At(0, PER_HEAD, h), h, before=h - 1)
            wo = At(FIRST_WO)
            split_hi(wo.plus(1))
            softmax(H - 1)
            take_v(H - 1)
            take_pT(H - 1)
            take_o(H - 1)
            act.wait_ge(pv_done, NH * H)
            act.wait_ge(pt_ready, PT_BANKS * H)
            for cb in range(NC):
                act.dma_start(xres[:, :, cb * BANK:(cb + 1) * BANK],
                              x_v[:, :, cb * BANK:(cb + 1) * BANK]).then_inc(x_in[cb], 16)
            act.dma_start(gain[:], norm_ffn.rearrange("a d -> (a d)").partition_broadcast(P)).then_inc(gain_in, 16)

            def squares(cb):
                for tb in range(NT):
                    act.wait_ge(added, NT * cb + tb + 1)
                    nc.scalar.activation(ps[:, YB[cb % 2][tb], :], xres[:, tb, cb * BANK:(cb + 1) * BANK],
                                         ACT.Square, accum_out=sumsq[:, tb, cb:cb + 1]).then_inc(sq_done, 1)

            split_hi(wo.plus(2))
            squares(0)
            split_hi(wo.plus(3))
            for cb in range(1, NC):
                split_hi(wo.plus(2 * cb + 2))
                squares(cb)
                if cb < NC - 1:
                    split_hi(wo.plus(2 * cb + 3))
            for tb in range(NT):
                take_hT(1, tb)
            split_hi(wo.plus(2 * NC + 1))
            act.wait_ge(h_ready, 4 * NT * 2)
            act.dma_start(gain[:], norm_out.partition_broadcast(P)).then_inc(gain_in, 16)

            def ffn(g, last=False):
                at = At(FIRST_FFN, FFN, g)
                for f in range(G):
                    wait_used(act, at.plus(2 * f))
                    nc.scalar.activation(tmp[:, f % 2, :], ps[:, 2 * (f % 2), :], ACT.Silu).then_inc(silu_done, 1)
                    split_hi(at.plus(2 * f + 2))
                    act.wait_ge(a_done, G * g + (f + 1))
                    nc.scalar.activation(oT[0][:, f, :], tmp[:, 2 + f % 2, :], ACT.Copy).then_inc(a_hi, 1)
                    split_hi(at.plus(2 * f + 3))
                for j in range(2 * G + 2, 3 * G if last else 3 * G + 2):
                    split_hi(at.plus(j))

            with act.Fori(0, GROUPS - 1) as g:
                ffn(g)
            ffn(GROUPS - 1, last=True)
            for tb in range(NT):
                act.wait_ge(added, NT * NC * (GROUPS + 1) - NT + tb + 1)
                act.wait_ge(sq_done, NT + NT * NC + tb)
                nc.scalar.activation(ps[:, 0:4, :], xres[:, tb, :].rearrange("p (c n) -> p c n", n=BANK),
                                     ACT.Square, accum_out=sumsq[:, tb, 0:1]).then_inc(sq_done, 1)

        @block.vector
        def _(dve):
            def split_lo(at):
                dve.wait_ge(hi_ready, at.count(1))
                nc.vector.tensor_tensor(split[1][:, at.ring, :], raw[:, at.raw, :],
                                        f32(split[0][:, at.ring, :]), ALU.subtract).then_inc(lo_ready, 1)

            def mean_square(norm, tb, parts, steps):
                source = sumsq[:, tb, 0:1]
                if parts > 1:
                    nc.vector.reduce_sum(var[:, tb:tb + 1], sumsq[:, tb, 0:parts], AX).then_inc(stat, 1)
                    steps += 1
                    dve.wait_ge(stat, steps)
                    source = var[:, tb:tb + 1]
                nc.vector.tensor_scalar(var[:, tb:tb + 1], source, 1.0 / D, RMS_EPS, ALU.mult,
                                        ALU.add).then_inc(var_ready, 1)

            def take_hT(norm, tb):
                for q in range(4):
                    n = 4 * NT * norm + 4 * tb + q
                    dve.wait_ge(hT_hi, n + 1)
                    nc.vector.tensor_tensor(hT[1][:, 4 * q:4 * q + 4, tb * P:(tb + 1) * P],
                                            ps[:, TP[norm][q], :].rearrange("p (c t) -> p c t", t=P),
                                            f32(hT[0][:, 4 * q:4 * q + 4, tb * P:(tb + 1) * P]),
                                            ALU.subtract).then_inc(hT_done, 1)

            def normalise(norm, tb):
                dve.wait_ge(rstd_ready, NT * norm + tb + 1)
                for q in range(4):
                    n = 4 * NT * norm + 4 * tb + q
                    if tb:
                        dve.wait_ge(h_turned, n - 3)
                    nc.vector.scalar_tensor_tensor(tmp[:, q, :], xres[:, tb, q * BANK:(q + 1) * BANK],
                                                   rstd[:, tb:tb + 1], gain[:, q * BANK:(q + 1) * BANK],
                                                   ALU.mult, ALU.mult).then_inc(h_ready, 1)

            def softmax(h):
                for tb in range(NT):
                    dve.wait_ge(s_done, NT * h + (tb + 1))
                    diag = ps[:, SC[tb], tb * P:(tb + 1) * P]
                    nc.vector.tensor_tensor(diag, diag, bound[:], ALU.min).then_inc(masked, 1)
                    dve.wait_ge(masked, NT * h + (tb + 1))
                    nc.vector.reduce_max(negmax[:, tb:tb + 1], ps[:, SC[tb], 0:(tb + 1) * P], AX,
                                         negate=True).then_inc(max_ready, 1)
                for tb in range(NT):
                    dve.wait_ge(exp_done, NT * h + (tb + 1))
                    nc.vector.reciprocal(rinv[:, tb:tb + 1], rowsum[:, tb:tb + 1]).then_inc(inv_ready, 1)
                    dve.wait_ge(inv_ready, NT * h + (tb + 1))
                    nc.vector.tensor_scalar(tmp_row(tb), tmp_row(tb), rinv[:, tb:tb + 1], None,
                                            ALU.mult).then_inc(p_ready, 1)

            def take_v(h):
                for b in range(2):
                    dve.wait_ge(v_hi, 2 * h + (b + 1))
                    nc.vector.tensor_tensor(v[1][:, 2 * b:2 * b + 2, :],
                                            ps[:, PVB[b], :].rearrange("p (t d) -> p t d", d=HD),
                                            f32(v[0][:, 2 * b:2 * b + 2, :]), ALU.subtract).then_inc(v_ready, 1)

            def take_pT(h):
                for b in range(PT_BANKS):
                    at = slice(b * BANK, b * BANK + pt_cols[b])
                    dve.wait_ge(pt_hi, PT_BANKS * h + (b + 1))
                    nc.vector.tensor_tensor(pT[1][:, at], ps[:, SC[b], 0:pt_cols[b]], f32(pT[0][:, at]),
                                            ALU.subtract).then_inc(pt_ready, 1)

            def take_o(h):
                for d in range(NH):
                    dve.wait_ge(o_hi, NH * h + (d + 1))
                    nc.vector.tensor_tensor(oT[1][:, h * NH + d, :], ps[:, PVB[d], :],
                                            f32(oT[0][:, h * NH + d, :]), ALU.subtract).then_inc(o_ready, 1)

            def take_qk(h, j):
                dve.wait_ge(qk_hi, QK * h + (j + 1))
                hi, lo = (part[:, j % NH, :] for part in qk[j // NH])
                nc.vector.scalar_tensor_tensor(lo, ps[:, PROJ[j % 2], :], SCALE if j < NH else 1.0, f32(hi),
                                               ALU.mult, ALU.subtract).then_inc(qk_done, 1)

            def head(at, h, head_col, before=None):
                fresh = before is None
                split_lo(at.plus(1))
                if not fresh:
                    softmax(before)
                take_qk(h, 0)
                nc.vector.tensor_scalar(decay_h[:], f32(decay_s[:]), head_col, None,
                                        ALU.mult).then_inc(decay_ready, 1)
                split_lo(at.plus(2))
                if not fresh:
                    take_v(before)
                take_qk(h, 1)
                split_lo(at.plus(3))
                if not fresh:
                    take_pT(before)
                take_qk(h, 2)
                split_lo(at.plus(4))
                if not fresh:
                    take_o(before)
                take_qk(h, 3)
                split_lo(at.plus(5))
                split_lo(at.plus(6))

            for tb in range(NT):
                dve.wait_ge(sq_done, tb + 1)
                mean_square(0, tb, 1, 0)
                if tb == 0:
                    dve.wait_ge(gain_in, 16)
                normalise(0, tb)
                if tb:
                    take_hT(0, tb - 1)
            take_hT(0, NT - 1)
            for r in range(4):
                dve.wait_ge(pad_hi, r + 1)
                nc.vector.tensor_tensor(pad(1)[:, :, r::32], wf[:], f32(pad(0)[:, :, r::32]),
                                        ALU.subtract).then_inc(pad_lo, 1)
            split_lo(At(0))
            nc.vector.reduce_sum(head_of[:], rows[:], AX).then_inc(stat, 1)
            nc.vector.reduce_sum(row_of[:, 0:4], rows[:].rearrange("p h r -> p r h"), AX).then_inc(stat, 1)
            dve.wait_ge(stat, 2)
            nc.vector.tensor_scalar(row_of[:, 6:8], row_of[:, 2:4], -1.0, None, ALU.mult).then_inc(stat, 1)
            nc.vector.tensor_tensor(row_of[:, 4:5], row_of[:, 0:1], row_of[:, 1:2], ALU.add).then_inc(stat, 1)
            nc.vector.tensor_tensor(row_of[:, 5:6], row_of[:, 2:3], row_of[:, 3:4], ALU.add).then_inc(stat, 1)
            z, soft, logs, cum, mixed = tmp[:, 0, :], tmp[:, 3, :], tmp[:, 1, :], tmp[:, 2, :], tmp[:, 3, :]
            dve.wait_ge(f_done, 1)
            nc.vector.tensor_scalar(z, ps[:, SC[0], :], bf[:, 0:1], None, ALU.add).then_inc(gate_v, 1)
            dve.wait_ge(gate_s, 3)
            nc.vector.scalar_tensor_tensor(logs, z, 0.0, soft, ALU.min, ALU.subtract).then_inc(gate_v, 1)
            dve.wait_ge(gate_v, 2)
            nc.vector.memset(z, 1.0).then_inc(gate_v, 1)
            dve.wait_ge(gate_v, 3)
            nc.vector.tensor_tensor_scan(cum, z, logs, 0.0, ALU.mult, ALU.add).then_inc(gate_v, 1)
            dve.wait_ge(gate_v, 4)
            nc.vector.tensor_copy(decay_h[:], cum).then_inc(gate_v, 1)
            dve.wait_ge(gate_v, 5)
            nc.vector.tensor_tensor(logs, cum, f32(decay_h[:]), ALU.subtract).then_inc(gate_v, 1)
            dve.wait_ge(stat, 5)
            nc.vector.tensor_scalar(mixed, f32(decay_h[:]), row_of[:, 0:1], row_of[:, 5:6], ALU.mult,
                                    ALU.add).then_inc(gate_v, 1)
            nc.vector.tensor_scalar(z, f32(decay_h[:]), row_of[:, 6:7], row_of[:, 4:5], ALU.mult,
                                    ALU.add).then_inc(gate_v, 1)
            dve.wait_ge(gate_v, 8)
            nc.vector.scalar_tensor_tensor(decay_t[:], logs, row_of[:, 1:2], mixed, ALU.mult,
                                           ALU.add).then_inc(gate_v, 1)
            nc.vector.scalar_tensor_tensor(decay_s[:], logs, row_of[:, 7:8], z, ALU.mult,
                                           ALU.add).then_inc(gate_v, 1)
            dve.wait_ge(gate_v, 10)
            head(At(0, PER_HEAD, 0), 0, head_of[:, 0:1])
            with dve.Fori(1, H) as h:
                head(At(0, PER_HEAD, h), h, head_of[:, bass.ds(h, 1)], before=h - 1)
            wo = At(FIRST_WO)
            split_lo(wo.plus(1))
            softmax(H - 1)
            take_v(H - 1)
            take_pT(H - 1)
            take_o(H - 1)

            def add(count, cb, bank, tb):
                dve.wait_ge(y_done, count)
                part = xres[:, tb, cb * BANK:(cb + 1) * BANK]
                nc.vector.tensor_tensor(part, ps[:, bank, :], part, ALU.add).then_inc(added, 1)

            split_lo(wo.plus(2))
            for cb in range(NC):
                dve.wait_ge(x_in[cb], 32)
                for tb in range(NT):
                    add(NT * cb + tb + 1, cb, YB[cb % 2][tb], tb)
                split_lo(wo.plus(2 * cb + 3)) if cb < NC - 1 else None
                split_lo(wo.plus(2 * cb + 4)) if cb < NC - 1 else None
            dve.wait_ge(gain_in, 32)
            for tb in range(NT):
                dve.wait_ge(sq_done, NT + NT * (NC - 1) + tb + 1)
                mean_square(1, tb, NC, 5 + tb)
                normalise(1, tb)
                if tb:
                    take_hT(1, tb - 1)
            take_hT(1, NT - 1)
            split_lo(wo.plus(2 * NC + 1))

            def ffn(g, last=False):
                at = At(FIRST_FFN, FFN, g)
                for f in range(G):
                    split_lo(at.plus(2 * f + 2))
                    dve.wait_ge(silu_done, G * g + (f + 1))
                    wait_used(dve, at.plus(2 * f + 1))
                    a = tmp[:, 2 + f % 2, :]
                    nc.vector.tensor_tensor(a, ps[:, 2 * (f % 2) + 1, :], tmp[:, f % 2, :],
                                            ALU.mult).then_inc(a_done, 1)
                    dve.wait_ge(a_hi, G * g + (f + 1))
                    nc.vector.tensor_tensor(oT[1][:, f, :], a, f32(oT[0][:, f, :]),
                                            ALU.subtract).then_inc(a_ready, 1)
                    split_lo(at.plus(2 * f + 3))
                for cb in range(NC):
                    for tb in range(NT):
                        add((NT * NC) * g + (NT * (NC + cb) + tb + 1), cb, SC[tb], tb)
                    if not (last and cb >= NC - 2):
                        split_lo(at.plus(2 * G + 2 + cb))

            with dve.Fori(0, GROUPS - 1) as g:
                ffn(g)
            ffn(GROUPS - 1, last=True)
            dve.wait_ge(gain_in, 48)
            for tb in range(NT):
                dve.wait_ge(sq_done, NT + NT * NC + tb + 1)
                mean_square(2, tb, 1, 0)
                dve.wait_ge(rstd_ready, 2 * NT + tb + 1)
                for c in range(0, D, D // 2):
                    part = xres[:, tb, c:c + D // 2]
                    nc.vector.scalar_tensor_tensor(part, part, rstd[:, tb:tb + 1], gain[:, c:c + D // 2],
                                                   ALU.mult, ALU.mult).then_inc(normed, 1)

        @block.tensor
        def _(pe):
            def products(bank, stationary, moving, tiles, first=True, last=True):
                for t in tiles:
                    for sp, mp in PASSES:
                        ins = nc.tensor.matmul(bank, stationary(sp, t), moving(mp, t),
                                               start=first and t == tiles[0] and (sp, mp) == PASSES[0],
                                               stop=last and t == tiles[-1] and (sp, mp) == PASSES[-1])
                return ins

            def turn(norm):
                for n in range(4 * NT):
                    q = n % 4
                    pe.wait_ge(h_ready, 4 * NT * norm + n + 1)
                    if n >= 4 or norm:
                        pe.wait_ge(hT_done, 4 * NT * norm + max(n - 3, 0))
                    for c in range(4):
                        ins = nc.tensor.transpose(ps[:, TP[norm][q], c * P:(c + 1) * P],
                                                  tmp[:, q, c * P:(c + 1) * P], ident[:])
                    ins.then_inc(h_turned, 1)

            def project(at, bank):
                pe.wait_ge(lo_ready, at.count(1))
                products(ps[:, bank, :], lambda part, k: slab(split, at, part, k, P),
                         lambda part, k: hT[part][:, k, :], range(ND)).then_inc(slab_used, 1)

            def scores(h):
                pe.wait_ge(decay_ready, h + 1)
                pe.wait_ge(qk_done, QK * h + QK)
                for tb in range(NT):
                    t, keys = slice(tb * P, (tb + 1) * P), (tb + 1) * P
                    bank = ps[:, SC[tb], 0:keys]
                    products(bank, lambda part, d: qk[0][part][:, d, t], lambda part, d: qk[1][part][:, d, 0:keys],
                             range(NH), last=False)
                    nc.tensor.matmul(bank, decay_t[:, t], decay_h[:, 0:keys], start=False,
                                     stop=True).then_inc(s_done, 1)

            def turn_v(h):
                pe.wait_ge(v_taken, VV * h + VV)
                for b in range(2):
                    for tb in (2 * b, 2 * b + 1):
                        for d in range(NH):
                            col = (tb % 2) * HD + d * P
                            ins = nc.tensor.transpose(ps[:, PVB[b], col:col + P], vT[:, d, tb * P:(tb + 1) * P],
                                                      ident[:])
                    ins.then_inc(vt_done, 1)

            def turn_p(h):
                pe.wait_ge(p_ready, NT * h + NT)
                for b in range(PT_BANKS):
                    for s in (s for s in pt_at if pt_at[s][0] == b):
                        for tb in range(s, NT):
                            col = pt_at[s][1] + (tb - s) * P
                            ins = nc.tensor.transpose(ps[:, SC[b], col:col + P],
                                                      tmp_row(tb)[:, s * P:(s + 1) * P], ident[:])
                    ins.then_inc(pt_done, 1)

            def weigh_v(h):
                pe.wait_ge(v_ready, 2 * h + 2)
                for n, s in enumerate(pt_at):
                    b, col = pt_at[s]
                    pe.wait_ge(pt_ready, PT_BANKS * h + (b + 1))
                    for d in range(NH):
                        ins = products(ps[:, PVB[d], s * P:S], lambda part, k: v[part][:, k, d * P:(d + 1) * P],
                                       lambda part, k: pT[part][:, b * BANK + col:b * BANK + col + S - k * P],
                                       [s], first=n == 0, last=n == NT - 1)
                        if n == NT - 1:
                            ins.then_inc(pv_done, 1)

            def head(at, h, before=None):
                fresh = before is None
                if not fresh:
                    scores(before)
                    pe.wait_ge(v_taken, VV * h - 1)
                project(at, PROJ[0])
                if not fresh:
                    turn_v(before)
                project(at.plus(1), PROJ[1])
                if not fresh:
                    turn_p(before)
                pe.wait_ge(qk_done, QK * h + 1)
                project(at.plus(2), PROJ[0])
                if not fresh:
                    weigh_v(before)
                for j in range(3, PER_HEAD):
                    pe.wait_ge(qk_done, QK * h + (j - 1))
                    project(at.plus(j), PROJ[j % 2])

            pe.wait_ge(const_set, CONSTS)
            turn(0)
            pe.wait_ge(pad_lo, 4)
            pe.wait_ge(hT_done, 4 * NT)
            padded = [pad(0), pad(1)]
            products(ps[:, SC[0], :], lambda part, k: padded[part][:, k, :], lambda part, k: hT[part][:, k, :],
                     range(ND)).then_inc(f_done, 1)
            head(At(0, PER_HEAD, 0), 0)
            with pe.Fori(1, H) as h:
                head(At(0, PER_HEAD, h), h, before=h - 1)

            wo = At(FIRST_WO)

            def mix(cb, tb, tiles, first=False, last=False):
                at = wo.plus(2 * cb)
                return products(ps[:, YB[cb % 2][tb], :], lambda part, k: oT[part][:, k, tb * P:(tb + 1) * P],
                                lambda part, k: slab(split, at.plus(k // 4), part, k % 4, BANK),
                                tiles, first=first, last=last)

            h = H - 1
            scores(h)
            pe.wait_ge(v_taken, VV * H)
            pe.wait_ge(lo_ready, wo.count(2))
            pe.wait_ge(o_ready, NH * h)
            early, late = range(0, NH * h), range(NH * h, NK)
            mix(0, 0, early, first=True)
            mix(0, 1, early, first=True)
            turn_v(h)
            turn_p(h)
            mix(0, 2, early, first=True)
            weigh_v(h)
            mix(0, 3, early[:4], first=True).then_inc(slab_used, 1)
            mix(0, 3, early[4:])
            pe.wait_ge(o_ready, NH * H)
            for tb in range(NT):
                ins = mix(0, tb, late, last=True)
                ins.then_inc(y_done, 1)
            for cb in range(1, NC):
                for part in range(2):
                    pe.wait_ge(lo_ready, wo.plus(2 * cb + part).count(1))
                    for tb in range(NT):
                        if part == 0 and cb >= 2:
                            pe.wait_ge(sq_done, NT + NT * (cb - 2) + tb + 1)
                        ins = mix(cb, tb, range(4 * part, 4 * part + 4), first=part == 0, last=part == 1)
                        if part == 1:
                            ins.then_inc(y_done, 1)
                    if part == 0:
                        ins.then_inc(slab_used, 1)
            turn(1)
            pe.wait_ge(hT_done, 4 * NT * 2)

            with pe.Fori(0, GROUPS) as g:
                at = At(FIRST_FFN, FFN, g)
                for f in range(G):
                    if f >= 2:
                        pe.wait_ge(a_ready, G * g + (f - 1))
                    project(at.plus(2 * f), 2 * (f % 2))
                    project(at.plus(2 * f + 1), 2 * (f % 2) + 1)

                def down(cb, tb, tiles, first=True, last=True):
                    a = at.plus(2 * G + cb)
                    return products(ps[:, SC[tb], :], lambda part, k: oT[part][:, k, tb * P:(tb + 1) * P],
                                    lambda part, k: slab(split, a, part, k, BANK), tiles, first=first, last=last)

                def bank_free(cb, tb):
                    pe.wait_ge(added, (NT * NC) * g + (NT * (NC + cb - 1) + tb + 1))

                pe.wait_ge(a_ready, G * g + (G - 1))
                pe.wait_ge(lo_ready, at.plus(2 * G).count(1))
                for tb in range(2):
                    bank_free(0, tb)
                    down(0, tb, range(G - 1), last=False)
                pe.wait_ge(a_ready, G * g + G)
                for tb in range(2):
                    down(0, tb, [G - 1], first=False).then_inc(y_done, 1)
                for cb in range(NC):
                    pe.wait_ge(lo_ready, at.plus(2 * G + cb).count(1))
                    for tb in range(NT):
                        if cb or tb >= 2:
                            bank_free(cb, tb)
                            down(cb, tb, range(G)).then_inc(y_done, 1)


_INS = ["x", "norm_mix", "fox_w_in", "fox_b_f", "fox_w_out", "norm_ffn", "ffn_w_gate_up", "ffn_w_down", "final_norm"]


def kernel(**inputs):
    import numpy as _np
    import concourse.bacc as _bacc
    from concourse import mybir as _mybir
    from concourse.bass_utils import run_bass_kernel_spmd as _run

    nc = _bacc.Bacc("TRN2", target_bir_lowering=False, num_devices=1)
    arrays, args = {}, []
    for name in _INS:
        a = _np.ascontiguousarray(inputs[name])
        arrays[f"in_{name}_dram"] = a
        args.append(nc.dram_tensor(f"in_{name}_dram", a.shape, _mybir.dt.from_np(a.dtype), kind="ExternalInput").ap())
    shape = tuple(inputs["x"].shape)
    args.append(nc.dram_tensor("out_0_dram", shape, _mybir.dt.float32, kind="ExternalOutput").ap())
    fox_layer(nc, *args)
    r = _run(nc, [arrays], core_ids=[0])
    return r.results[0]["out_0_dram"]
```

```python
from contextlib import ExitStack

import concourse.bass as bass
from concourse import mybir

F32 = mybir.dt.float32
F32R = mybir.dt.float32r
ALU = mybir.AluOpType
ACT = mybir.ActivationFunctionType
AX = mybir.AxisListType.X

P = 128
SLAB = 2048
RAW = 3
RING = 2
BANK = 512
RMS_EPS = 1e-6
FLT_MAX = 3.4028234e38
QK, VV = 4, 2
PER_HEAD = QK + VV
PASSES = ((0, 0), (0, 1), (1, 0))


class At:

    def __init__(self, off, per=0, i=0):
        assert per % (RAW * RING) == 0
        self.off, self.per, self.i = off, per, i
        self.raw, self.ring = off % RAW, off % RING

    def count(self, more=0):
        return self.per * self.i + (self.off + more)

    def landed(self):
        return (16 * (self.per // RAW)) * self.i + 16 * (self.off // RAW + 1)

    def plus(self, j):
        return At(self.off + j, self.per, self.i)


def fox_layer(nc, x, norm_mix, w_in, b_f, w_out, norm_ffn, w_gu, w_down, norm_out, out):
    _, S, D = x.shape
    H = b_f.shape[1]
    A = w_out.shape[1]
    HD = A // H
    F = w_down.shape[1]
    NT, ND = S // P, D // P
    NH = HD // P
    NK = A // P
    NC = D // BANK
    OWN = (3, 2, 3)
    G = 4
    GROUPS = F // P // G
    FFN = 3 * G
    SCALE = HD ** -0.5
    FIRST_WO = PER_HEAD * H
    FIRST_FFN = FIRST_WO + 2 * NC
    SLABS = FIRST_FFN + FFN * GROUPS
    TRI = NT * (NT + 1) // 2 * P
    assert S == BANK and ND * P == SLAB and NC == NT == G == 4 and NH == 2 and GROUPS * G * P == F
    assert FIRST_FFN % RING == 0 and SCALE == 2.0 ** -4
    p_at = [tb * (tb + 1) // 2 * P for tb in range(NT)]
    pt_at = {0: (0, 0), 1: (1, 0), 3: (1, 3 * P), 2: (2, 0)}
    pt_cols = [BANK, BANK, 2 * P]
    PT_BANKS = len(pt_cols)

    x_v = x.rearrange("a (t p) d -> p (a t) d", p=P)
    out_v = out.rearrange("a (t p) d -> p (a t) d", p=P)
    w_in_v = w_in.rearrange("a (c p) n -> p (a c) n", p=P)
    w_out_v = w_out.rearrange("a (k p) n -> p (a k) n", p=P)
    w_gu_v = w_gu.rearrange("a (c p) n -> p (a c) n", p=P)
    w_down_v = w_down.rearrange("a (f p) n -> p (a f) n", p=P)

    with ExitStack() as ctx:
        def sb(name, shape, dt=F32):
            return ctx.enter_context(nc.sbuf_tensor(name, shape, dt))

        def sem(name):
            return ctx.enter_context(nc.semaphore(name))

        hT = [sb(f"hT_{n}", [P, ND, S], F32R) for n in ("hi", "lo")]
        split = [sb(f"split_{n}", [P, RING, SLAB], F32R) for n in ("hi", "lo")]
        raw = sb("raw", [P, RAW, SLAB])
        oT = [sb(f"oT_{n}", [P, NK, S], F32R) for n in ("hi", "lo")]
        tmp = sb("tmp", [P, 4, BANK])
        ident = sb("ident", [P, P])
        bound = sb("bound", [P, P])
        with nc.sbuf_tensor("xres", [P, NT, D], F32) as xres, nc.sbuf_tensor("gain", [P, D], F32) as gain:
            pass
        qk = [[sb(f"{w}T_{n}", [P, NH, S], F32R) for n in ("hi", "lo")] for w in "qk"]
        v = [sb(f"v_{n}", [P, NT, HD], F32R) for n in ("hi", "lo")]
        pT = [sb(f"pT_{n}", [P, TRI], F32R) for n in ("hi", "lo")]
        vT = sb("vT", [P, NH, S])
        decay_t = sb("decay_t", [P, S], F32R)
        decay_s = sb("decay_s", [P, S], F32R)
        decay_h = sb("decay_h", [P, S], F32R)
        rows = sb("rows", [P, H, 4])
        row_of = sb("row_of", [P, 8])
        head_of = sb("head_of", [P, H])
        wf = sb("wf", [P, ND, H])
        bf_all = sb("bf_all", [P, H])
        bf = sb("bf", [P, 1])
        half = sb("half", [P, 1])
        sumsq = sb("sumsq", [P, NT, NC])
        pairs = sb("pairs", [P, 2])
        var = sb("var", [P, NT])
        rstd = sb("rstd", [P, NT])
        negmax = sb("negmax", [P, NT])
        rowsum = sb("rowsum", [P, NT])
        rinv = sb("rinv", [P, NT])

        ps = ctx.enter_context(nc.psum_tensor("ps", [P, 8, BANK], F32))
        PROJ = (0, 1)
        PVB = (2, 3)
        GATE = PVB[0]
        SC = (4, 5, 6, 7)
        YB = ((0, 1, 7, 4), (2, 3, 5, 6))
        GU = ((2, 3), (0, 1))
        TP = (SC, YB[0])

        x_in = [sem(f"x_in{i}") for i in range(NT)]
        gain_in = sem("gain_in")
        wf_in = sem("wf_in")
        bf_in = sem("bf_in")
        raw_in = [sem(f"raw_in{i}") for i in range(RAW)]
        out_done = sem("out_done")
        hi_ready = sem("hi_ready")
        lo_ready = sem("lo_ready")
        slab_used = sem("slab_used")
        const_set = sem("const_set")
        sq_done = sem("sq_done")
        stat = sem("stat")
        var_step = sem("var_step")
        rstd_ready = sem("rstd_ready")
        h_ready = sem("h_ready")
        scaled = sem("scaled")
        h_pool = sem("h_pool")
        h_turned = sem("h_turned")
        hT_hi = sem("hT_hi")
        hT_done = sem("hT_done")
        pad_hi = sem("pad_hi")
        pad_lo = sem("pad_lo")
        f_done = sem("f_done")
        gate_v = sem("gate_v")
        gate_s = sem("gate_s")
        qk_hi = sem("qk_hi")
        qk_done = sem("qk_done")
        v_taken = sem("v_taken")
        decay_ready = sem("decay_ready")
        s_done = sem("s_done")
        masked = sem("masked")
        max_ready = sem("max_ready")
        exp_done = sem("exp_done")
        inv_ready = sem("inv_ready")
        p_ready = sem("p_ready")
        vt_done = sem("vt_done")
        v_hi = sem("v_hi")
        v_ready = sem("v_ready")
        pt_done = sem("pt_done")
        pt_hi = sem("pt_hi")
        pt_ready = sem("pt_ready")
        pv_done = sem("pv_done")
        o_hi = sem("o_hi")
        o_ready = sem("o_ready")
        y_done = sem("y_done")
        added = sem("added")
        silu_done = sem("silu_done")
        a_done = sem("a_done")
        a_hi = sem("a_hi")
        a_ready = sem("a_ready")

        block = ctx.enter_context(nc.Block())

        def f32(ap):
            return ap.bitcast(F32)

        def tmp_row(tb):
            return tmp[:, :, :].rearrange("p a b -> p (a b)")[:, p_at[tb]:p_at[tb] + (tb + 1) * P]

        def pad(part):
            return oT[0][:, part * 4:(part + 1) * 4, :].rearrange("p a b -> p (a b)").rearrange(
                "p (k n) -> p k n", n=P)

        def own_chunks(norm, tb, q):
            return NT * sum(OWN[:norm]) + OWN[norm] * tb + q + 1

        def shared_chunks(norm, tb, q):
            return NT * (norm * NC - sum(OWN[:norm])) + (NC - OWN[norm]) * tb + q - OWN[norm] + 1

        def wait_normalised(eng, norm, tb, q):
            if q < OWN[norm]:
                eng.wait_ge(h_ready, own_chunks(norm, tb, q))
            else:
                eng.wait_ge(h_pool, shared_chunks(norm, tb, q))

        def chunk_of(norm, tb, q):
            return tmp[:, q, :] if norm < 2 else xres[:, tb, q * BANK:(q + 1) * BANK]

        def wait_used(eng, at):
            n = at.off
            if n < FIRST_WO:
                eng.wait_ge(slab_used, at.per * at.i + (n + 1))
            elif n < FIRST_FFN:
                cb, second = divmod(n - FIRST_WO, 2)
                if second:
                    eng.wait_ge(y_done, NT * (cb + 1))
                else:
                    eng.wait_ge(slab_used, FIRST_WO + cb + 1)
            else:
                j = n - FIRST_FFN
                if j < 2 * G:
                    eng.wait_ge(slab_used, (2 * G) * at.i + (FIRST_WO + NC + j + 1))
                else:
                    eng.wait_ge(y_done, (NT * NC) * at.i + (NT * NC + NT * (j - 2 * G + 1)))

        def slab(parts, at, part, tile, cols):
            return parts[part][:, at.ring, tile * cols:(tile + 1) * cols]

        @block.sync
        def _(sp):
            def load(at, view, source, first=False):
                if not first:
                    sp.wait_ge(lo_ready, at.count(1 - RAW))
                sp.dma_start(view, source).then_inc(raw_in[at.raw], 16)

            def tile_of(at, cols):
                return raw[:, at.raw, :].rearrange("p (k n) -> p k n", n=cols)

            def load_head(h):
                at = At(0, PER_HEAD, h)
                for j in range(PER_HEAD):
                    a = at.plus(j)
                    col = h * HD + ((j // NH) * A + (j % NH) * P)
                    load(a, tile_of(a, P), w_in_v[:, :, bass.ds(col, P)],
                         first=isinstance(h, int) and j < RAW)

            for tb in range(NT):
                sp.dma_start(xres[:, tb, :], x_v[:, tb, :]).then_inc(x_in[tb], 16)
                if tb == 0:
                    sp.dma_start(gain[:], norm_mix.rearrange("a d -> (a d)").partition_broadcast(P)
                                 ).then_inc(gain_in, 16)
            with nc.allow_non_contiguous_dma(reason="the gate's four columns"):
                sp.dma_start(wf[:], w_in_v[:, :, 3 * A:3 * A + H]).then_inc(wf_in, 16)
            sp.dma_start(bf_all[:], b_f.rearrange("a h -> (a h)").partition_broadcast(P)).then_inc(bf_in, 16)
            load_head(0)
            with sp.Fori(1, H) as h:
                load_head(h)
            for j in range(2 * NC):
                a = At(FIRST_WO + j)
                cb, kt = j // 2, (j % 2) * (NK // 2)
                load(a, tile_of(a, BANK), w_out_v[:, kt:kt + NK // 2, cb * BANK:(cb + 1) * BANK])
            with sp.Fori(0, GROUPS) as g:
                at = At(FIRST_FFN, FFN, g)
                for j in range(2 * G):
                    a = at.plus(j)
                    load(a, tile_of(a, P), w_gu_v[:, :, bass.ds(g * (G * P) + ((j // 2) * P + (j % 2) * F), P)])
                for cb in range(NC):
                    a = at.plus(2 * G + cb)
                    load(a, tile_of(a, BANK), w_down_v[:, bass.ds(g * G, G), cb * BANK:(cb + 1) * BANK])
            for tb in range(NT):
                for q in range(NC):
                    wait_normalised(sp, 2, tb, q)
                    sp.dma_start(out_v[:, tb, q * BANK:(q + 1) * BANK], chunk_of(2, tb, q)).then_inc(out_done, 16)
            sp.wait_ge(out_done, 16 * NT * NC)

        @block.gpsimd
        def _(pool):
            nc.gpsimd.memset(half[:], -0.5).then_inc(const_set, 1)
            nc.gpsimd.memset(ident[:], 0.0).then_inc(const_set, 1)
            nc.gpsimd.memset(bound[:], FLT_MAX).then_inc(const_set, 1)
            nc.gpsimd.memset(rows[:], 0.0).then_inc(const_set, 1)
            pool.wait_ge(const_set, 4)
            nc.gpsimd.affine_select(out=ident[:], in_=ident[:], compare_op=ALU.not_equal, fill=1.0, base=0,
                                    pattern=[[-1, P]], channel_multiplier=1).then_inc(const_set, 1)
            for part in range(2):
                nc.gpsimd.memset(oT[0][:, part * 4:(part + 1) * 4, :].bitcast(F32), 0.0).then_inc(const_set, 1)
            nc.gpsimd.affine_select(out=bound[:], in_=bound[:], compare_op=ALU.is_ge, fill=-FLT_MAX, base=0,
                                    pattern=[[-1, P]], channel_multiplier=1).then_inc(const_set, 1)
            nc.gpsimd.affine_select(out=rows[:], in_=rows[:], compare_op=ALU.not_equal, fill=1.0, base=0,
                                    pattern=[[-32, H], [-1, 4]], channel_multiplier=1).then_inc(const_set, 1)
            steps = 0

            def step(ins):
                nonlocal steps
                steps += 1
                ins.then_inc(var_step, 1)
                pool.wait_ge(var_step, steps)

            for norm in range(3):
                for tb in range(NT):
                    v1 = var[:, tb:tb + 1]
                    if norm == 0:
                        pool.wait_ge(sq_done, tb + 1)
                        total = sumsq[:, tb, 0:1]
                    else:
                        pool.wait_ge(sq_done, NT + NT * NC * norm - NT + tb + 1)
                        step(nc.gpsimd.tensor_tensor(out=pairs[:], in0=sumsq[:, tb, 0:2], in1=sumsq[:, tb, 2:4],
                                                     op=ALU.add))
                        step(nc.gpsimd.tensor_tensor(out=v1, in0=pairs[:, 0:1], in1=pairs[:, 1:2], op=ALU.add))
                        total = v1
                    step(nc.gpsimd.tensor_scalar(v1, total, 1.0 / D, RMS_EPS, ALU.mult, ALU.add))
                    nc.gpsimd.tensor_tensor(out=rstd[:, tb:tb + 1], in0=v1, in1=half[:],
                                            op=ALU.pow).then_inc(rstd_ready, 1)
                    if tb == 0:
                        pool.wait_ge(gain_in, 16 * (norm + 1))
                    for q in range(OWN[norm], NC):
                        pool.wait_ge(scaled, shared_chunks(norm, tb, q))
                        nc.gpsimd.tensor_tensor(out=chunk_of(norm, tb, q), in0=chunk_of(norm, tb, q),
                                                in1=gain[:, q * BANK:(q + 1) * BANK],
                                                op=ALU.mult).then_inc(h_pool, 1)

        CONSTS = 9

        @block.scalar
        def _(act):
            def split_hi(at, first=False):
                act.wait_ge(raw_in[at.raw], at.landed())
                if not first:
                    wait_used(act, at.plus(-RING))
                nc.scalar.activation(split[0][:, at.ring, :], raw[:, at.raw, :], ACT.Copy).then_inc(hi_ready, 1)

            def take_hT(norm, tb):
                for q in range(4):
                    act.wait_ge(h_turned, 4 * NT * norm + 4 * tb + q + 1)
                    nc.scalar.activation(hT[0][:, 4 * q:4 * q + 4, tb * P:(tb + 1) * P],
                                         ps[:, TP[norm][q], :].rearrange("p (c t) -> p c t", t=P),
                                         ACT.Copy).then_inc(hT_hi, 1)

            def scale(norm, tb):
                act.wait_ge(rstd_ready, NT * norm + tb + 1)
                for q in range(OWN[norm], NC):
                    if norm < 2 and tb:
                        act.wait_ge(h_turned, 4 * NT * norm + 4 * tb + q - 3)
                    nc.scalar.activation(chunk_of(norm, tb, q), xres[:, tb, q * BANK:(q + 1) * BANK], ACT.Copy,
                                         scale=rstd[:, tb:tb + 1]).then_inc(scaled, 1)

            def softmax(h):
                for tb in range(NT):
                    act.wait_ge(max_ready, NT * h + (tb + 1))
                    nc.scalar.activation(tmp_row(tb), ps[:, SC[tb], 0:(tb + 1) * P], ACT.Exp,
                                         bias=negmax[:, tb:tb + 1],
                                         accum_out=rowsum[:, tb:tb + 1]).then_inc(exp_done, 1)

            def take_v(h):
                for b in range(2):
                    act.wait_ge(vt_done, 2 * h + (b + 1))
                    nc.scalar.activation(v[0][:, 2 * b:2 * b + 2, :],
                                         ps[:, PVB[b], :].rearrange("p (t d) -> p t d", d=HD),
                                         ACT.Copy).then_inc(v_hi, 1)

            def take_pT(h):
                for b in range(PT_BANKS):
                    act.wait_ge(pt_done, PT_BANKS * h + (b + 1))
                    nc.scalar.activation(pT[0][:, b * BANK:b * BANK + pt_cols[b]], ps[:, SC[b], 0:pt_cols[b]],
                                         ACT.Copy).then_inc(pt_hi, 1)

            def take_o(h):
                for d in range(NH):
                    act.wait_ge(pv_done, NH * h + (d + 1))
                    nc.scalar.activation(oT[0][:, h * NH + d, :], ps[:, PVB[d], :], ACT.Copy).then_inc(o_hi, 1)

            def take_qk(h, at, j):
                wait_used(act, at.plus(j))
                nc.scalar.activation(qk[j // NH][0][:, j % NH, :], ps[:, PROJ[j % 2], :], ACT.Copy,
                                     scale=SCALE if j < NH else 1.0).then_inc(qk_hi, 1)

            def head(at, h, before=None):
                fresh = before is None
                if not fresh:
                    split_hi(at.plus(1))
                    softmax(before)
                take_qk(h, at, 0)
                split_hi(at.plus(2))
                if not fresh:
                    take_v(before)
                take_qk(h, at, 1)
                split_hi(at.plus(3))
                if not fresh:
                    take_pT(before)
                take_qk(h, at, 2)
                split_hi(at.plus(4))
                if not fresh:
                    take_o(before)
                take_qk(h, at, 3)
                split_hi(at.plus(5))
                for j in range(VV):
                    wait_used(act, at.plus(QK + j))
                    nc.scalar.activation(vT[:, j, :], ps[:, PROJ[j % 2], :], ACT.Copy).then_inc(v_taken, 1)
                    if j == 0:
                        split_hi(at.plus(6))

            for tb in range(NT):
                act.wait_ge(x_in[tb], 16)
                if tb:
                    act.wait_ge(sq_done, tb)
                nc.scalar.activation(ps[:, 0:4, :], xres[:, tb, :].rearrange("p (c n) -> p c n", n=BANK),
                                     ACT.Square, accum_out=sumsq[:, tb, 0:1]).then_inc(sq_done, 1)
                if tb:
                    take_hT(0, tb - 1)
                scale(0, tb)
            act.wait_ge(wf_in, 16)
            act.wait_ge(const_set, CONSTS)
            for r in range(4):
                nc.scalar.activation(pad(0)[:, :, r::32], wf[:], ACT.Copy).then_inc(pad_hi, 1)
            split_hi(At(0), first=True)
            take_hT(0, NT - 1)
            split_hi(At(1), first=True)
            act.wait_ge(gate_v, 1)
            nc.scalar.activation(tmp[:, 1, :], tmp[:, 0, :], ACT.Abs).then_inc(gate_s, 1)
            act.wait_ge(gate_s, 1)
            nc.scalar.activation(tmp[:, 2, :], tmp[:, 1, :], ACT.Exp, scale=-1.0).then_inc(gate_s, 1)
            act.wait_ge(gate_s, 2)
            nc.scalar.activation(tmp[:, 3, :], tmp[:, 2, :], ACT.Ln, bias=1.0).then_inc(gate_s, 1)
            head(At(0, PER_HEAD, 0), 0)
            with act.Fori(1, H) as h:
                head(At(0, PER_HEAD, h), h, before=h - 1)
            wo = At(FIRST_WO)
            split_hi(wo.plus(1))
            softmax(H - 1)
            take_v(H - 1)
            take_pT(H - 1)
            take_o(H - 1)
            act.wait_ge(pv_done, NH * H)
            act.wait_ge(pt_ready, PT_BANKS * H)
            for cb in range(NC):
                act.dma_start(xres[:, :, cb * BANK:(cb + 1) * BANK],
                              x_v[:, :, cb * BANK:(cb + 1) * BANK]).then_inc(x_in[cb], 16)
            act.dma_start(gain[:], norm_ffn.rearrange("a d -> (a d)").partition_broadcast(P)).then_inc(gain_in, 16)

            def square(cb, tb, scratch, before=0):
                act.wait_ge(added, NT * NC * before + NT * cb + tb + 1)
                nc.scalar.activation(ps[:, scratch, :], xres[:, tb, cb * BANK:(cb + 1) * BANK],
                                     ACT.Square, accum_out=sumsq[:, tb, cb:cb + 1]).then_inc(sq_done, 1)

            split_hi(wo.plus(2))
            for cb in range(NC - 1):
                for tb in range(NT):
                    square(cb, tb, YB[cb % 2][tb])
                split_hi(wo.plus(2 * cb + 3))
                split_hi(wo.plus(2 * cb + 4))
            last = NC - 1
            square(last, 0, YB[last % 2][0])
            square(last, 1, YB[last % 2][1])
            scale(1, 0)
            square(last, 2, YB[last % 2][2])
            take_hT(1, 0)
            scale(1, 1)
            square(last, 3, YB[last % 2][3])
            take_hT(1, 1)
            scale(1, 2)
            take_hT(1, 2)
            scale(1, 3)
            split_hi(wo.plus(2 * NC + 1))
            take_hT(1, 3)
            wait_normalised(act, 1, NT - 1, OWN[1] - 1)
            wait_normalised(act, 1, NT - 1, NC - 1)
            act.dma_start(gain[:], norm_out.partition_broadcast(P)).then_inc(gain_in, 16)

            def ffn(g, last=False):
                at = At(FIRST_FFN, FFN, g)
                for f in range(G):
                    wait_used(act, at.plus(2 * f))
                    nc.scalar.activation(tmp[:, f % 2, :], ps[:, GU[f % 2][0], :], ACT.Silu).then_inc(silu_done, 1)
                    split_hi(at.plus(2 * f + 2))
                    act.wait_ge(a_done, G * g + (f + 1))
                    nc.scalar.activation(oT[0][:, f, :], tmp[:, 2 + f % 2, :], ACT.Copy).then_inc(a_hi, 1)
                    split_hi(at.plus(2 * f + 3))
                for cb in range(NC):
                    if not last or cb < NC - 2:
                        split_hi(at.plus(2 * G + 2 + cb))
                    if last:
                        for tb in range(NT):
                            if cb:
                                act.wait_ge(sq_done, NT + NT * NC + NT * (cb - 1) + tb + 1)
                            square(cb, tb, tb, before=GROUPS)
                            if cb == NC - 1 and tb:
                                scale(2, tb - 1)

            with act.Fori(0, GROUPS - 1) as g:
                ffn(g)
            ffn(GROUPS - 1, last=True)
            scale(2, NT - 1)

        @block.vector
        def _(dve):
            def split_lo(at):
                dve.wait_ge(hi_ready, at.count(1))
                nc.vector.tensor_tensor(split[1][:, at.ring, :], raw[:, at.raw, :],
                                        f32(split[0][:, at.ring, :]), ALU.subtract).then_inc(lo_ready, 1)

            def take_hT(norm, tb):
                for q in range(4):
                    n = 4 * NT * norm + 4 * tb + q
                    dve.wait_ge(hT_hi, n + 1)
                    nc.vector.tensor_tensor(hT[1][:, 4 * q:4 * q + 4, tb * P:(tb + 1) * P],
                                            ps[:, TP[norm][q], :].rearrange("p (c t) -> p c t", t=P),
                                            f32(hT[0][:, 4 * q:4 * q + 4, tb * P:(tb + 1) * P]),
                                            ALU.subtract).then_inc(hT_done, 1)

            def normalise(norm, tb):
                dve.wait_ge(rstd_ready, NT * norm + tb + 1)
                if tb == 0:
                    dve.wait_ge(gain_in, 16 * (norm + 1))
                for q in range(OWN[norm]):
                    if norm < 2 and tb:
                        dve.wait_ge(h_turned, 4 * NT * norm + 4 * tb + q - 3)
                    nc.vector.scalar_tensor_tensor(chunk_of(norm, tb, q), xres[:, tb, q * BANK:(q + 1) * BANK],
                                                   rstd[:, tb:tb + 1], gain[:, q * BANK:(q + 1) * BANK],
                                                   ALU.mult, ALU.mult).then_inc(h_ready, 1)

            def softmax(h):
                for tb in range(NT):
                    dve.wait_ge(s_done, NT * h + (tb + 1))
                    diag = ps[:, SC[tb], tb * P:(tb + 1) * P]
                    nc.vector.tensor_tensor(diag, diag, bound[:], ALU.min).then_inc(masked, 1)
                    dve.wait_ge(masked, NT * h + (tb + 1))
                    nc.vector.reduce_max(negmax[:, tb:tb + 1], ps[:, SC[tb], 0:(tb + 1) * P], AX,
                                         negate=True).then_inc(max_ready, 1)
                for tb in range(NT):
                    dve.wait_ge(exp_done, NT * h + (tb + 1))
                    nc.vector.reciprocal(rinv[:, tb:tb + 1], rowsum[:, tb:tb + 1]).then_inc(inv_ready, 1)
                    dve.wait_ge(inv_ready, NT * h + (tb + 1))
                    nc.vector.tensor_scalar(tmp_row(tb), tmp_row(tb), rinv[:, tb:tb + 1], None,
                                            ALU.mult).then_inc(p_ready, 1)

            def take_v(h):
                for b in range(2):
                    dve.wait_ge(v_hi, 2 * h + (b + 1))
                    nc.vector.tensor_tensor(v[1][:, 2 * b:2 * b + 2, :],
                                            ps[:, PVB[b], :].rearrange("p (t d) -> p t d", d=HD),
                                            f32(v[0][:, 2 * b:2 * b + 2, :]), ALU.subtract).then_inc(v_ready, 1)

            def take_pT(h):
                for b in range(PT_BANKS):
                    at = slice(b * BANK, b * BANK + pt_cols[b])
                    dve.wait_ge(pt_hi, PT_BANKS * h + (b + 1))
                    nc.vector.tensor_tensor(pT[1][:, at], ps[:, SC[b], 0:pt_cols[b]], f32(pT[0][:, at]),
                                            ALU.subtract).then_inc(pt_ready, 1)

            def take_o(h):
                for d in range(NH):
                    dve.wait_ge(o_hi, NH * h + (d + 1))
                    nc.vector.tensor_tensor(oT[1][:, h * NH + d, :], ps[:, PVB[d], :],
                                            f32(oT[0][:, h * NH + d, :]), ALU.subtract).then_inc(o_ready, 1)

            def take_qk(h, j):
                dve.wait_ge(qk_hi, QK * h + (j + 1))
                hi, lo = (part[:, j % NH, :] for part in qk[j // NH])
                nc.vector.scalar_tensor_tensor(lo, ps[:, PROJ[j % 2], :], SCALE if j < NH else 1.0, f32(hi),
                                               ALU.mult, ALU.subtract).then_inc(qk_done, 1)

            def head(at, h, head_col, before=None):
                fresh = before is None
                if not fresh:
                    split_lo(at.plus(1))
                    softmax(before)
                take_qk(h, 0)
                nc.vector.tensor_scalar(decay_h[:], f32(decay_s[:]), head_col, None,
                                        ALU.mult).then_inc(decay_ready, 1)
                split_lo(at.plus(2))
                if not fresh:
                    take_v(before)
                take_qk(h, 1)
                split_lo(at.plus(3))
                if not fresh:
                    take_pT(before)
                take_qk(h, 2)
                split_lo(at.plus(4))
                if not fresh:
                    take_o(before)
                take_qk(h, 3)
                split_lo(at.plus(5))
                split_lo(at.plus(6))

            for tb in range(NT):
                normalise(0, tb)
                if tb:
                    take_hT(0, tb - 1)
            for r in range(4):
                dve.wait_ge(pad_hi, r + 1)
                nc.vector.tensor_tensor(pad(1)[:, :, r::32], wf[:], f32(pad(0)[:, :, r::32]),
                                        ALU.subtract).then_inc(pad_lo, 1)
            split_lo(At(0))
            take_hT(0, NT - 1)
            split_lo(At(1))
            nc.vector.reduce_sum(head_of[:], rows[:], AX).then_inc(stat, 1)
            nc.vector.reduce_sum(row_of[:, 0:4], rows[:].rearrange("p h r -> p r h"), AX).then_inc(stat, 1)
            dve.wait_ge(stat, 2)
            nc.vector.tensor_scalar(row_of[:, 6:8], row_of[:, 2:4], -1.0, None, ALU.mult).then_inc(stat, 1)
            nc.vector.tensor_tensor(row_of[:, 4:5], row_of[:, 0:1], row_of[:, 1:2], ALU.add).then_inc(stat, 1)
            nc.vector.tensor_tensor(row_of[:, 5:6], row_of[:, 2:3], row_of[:, 3:4], ALU.add).then_inc(stat, 1)
            z, soft, logs, cum, mixed = tmp[:, 0, :], tmp[:, 3, :], tmp[:, 1, :], tmp[:, 2, :], tmp[:, 3, :]
            dve.wait_ge(bf_in, 16)
            nc.vector.tensor_tensor(bf_all[:], bf_all[:], head_of[:], ALU.mult).then_inc(stat, 1)
            dve.wait_ge(stat, 6)
            nc.vector.reduce_sum(bf[:], bf_all[:], AX).then_inc(stat, 1)
            dve.wait_ge(stat, 7)
            dve.wait_ge(f_done, 1)
            nc.vector.tensor_scalar(z, ps[:, GATE, :], bf[:, 0:1], None, ALU.add).then_inc(gate_v, 1)
            dve.wait_ge(gate_s, 3)
            nc.vector.scalar_tensor_tensor(logs, z, 0.0, soft, ALU.min, ALU.subtract).then_inc(gate_v, 1)
            dve.wait_ge(gate_v, 2)
            nc.vector.memset(z, 1.0).then_inc(gate_v, 1)
            dve.wait_ge(gate_v, 3)
            nc.vector.tensor_tensor_scan(cum, z, logs, 0.0, ALU.mult, ALU.add).then_inc(gate_v, 1)
            dve.wait_ge(gate_v, 4)
            nc.vector.tensor_copy(decay_h[:], cum).then_inc(gate_v, 1)
            dve.wait_ge(gate_v, 5)
            nc.vector.tensor_tensor(logs, cum, f32(decay_h[:]), ALU.subtract).then_inc(gate_v, 1)
            dve.wait_ge(stat, 5)
            nc.vector.tensor_scalar(mixed, f32(decay_h[:]), row_of[:, 0:1], row_of[:, 5:6], ALU.mult,
                                    ALU.add).then_inc(gate_v, 1)
            nc.vector.tensor_scalar(z, f32(decay_h[:]), row_of[:, 6:7], row_of[:, 4:5], ALU.mult,
                                    ALU.add).then_inc(gate_v, 1)
            dve.wait_ge(gate_v, 8)
            nc.vector.scalar_tensor_tensor(decay_t[:], logs, row_of[:, 1:2], mixed, ALU.mult,
                                           ALU.add).then_inc(gate_v, 1)
            nc.vector.scalar_tensor_tensor(decay_s[:], logs, row_of[:, 7:8], z, ALU.mult,
                                           ALU.add).then_inc(gate_v, 1)
            dve.wait_ge(gate_v, 10)
            head(At(0, PER_HEAD, 0), 0, head_of[:, 0:1])
            with dve.Fori(1, H) as h:
                head(At(0, PER_HEAD, h), h, head_of[:, bass.ds(h, 1)], before=h - 1)
            wo = At(FIRST_WO)
            split_lo(wo.plus(1))
            softmax(H - 1)
            take_v(H - 1)
            take_pT(H - 1)
            take_o(H - 1)

            def add(count, cb, bank, tb):
                dve.wait_ge(y_done, count)
                part = xres[:, tb, cb * BANK:(cb + 1) * BANK]
                nc.vector.tensor_tensor(part, ps[:, bank, :], part, ALU.add).then_inc(added, 1)

            split_lo(wo.plus(2))
            for cb in range(NC - 1):
                dve.wait_ge(x_in[cb], 32)
                for tb in range(NT):
                    add(NT * cb + tb + 1, cb, YB[cb % 2][tb], tb)
                split_lo(wo.plus(2 * cb + 3))
                split_lo(wo.plus(2 * cb + 4))
            cb = NC - 1
            dve.wait_ge(x_in[cb], 32)
            for tb in range(NT):
                add(NT * cb + tb + 1, cb, YB[cb % 2][tb], tb)
                if tb >= 1:
                    normalise(1, tb - 1)
                if tb >= 2:
                    take_hT(1, tb - 2)
            normalise(1, NT - 1)
            take_hT(1, NT - 2)
            split_lo(wo.plus(2 * NC + 1))
            take_hT(1, NT - 1)

            def ffn(g, last=False):
                at = At(FIRST_FFN, FFN, g)
                for f in range(G):
                    split_lo(at.plus(2 * f + 2))
                    dve.wait_ge(silu_done, G * g + (f + 1))
                    wait_used(dve, at.plus(2 * f + 1))
                    a = tmp[:, 2 + f % 2, :]
                    nc.vector.tensor_tensor(a, ps[:, GU[f % 2][1], :], tmp[:, f % 2, :],
                                            ALU.mult).then_inc(a_done, 1)
                    dve.wait_ge(a_hi, G * g + (f + 1))
                    nc.vector.tensor_tensor(oT[1][:, f, :], a, f32(oT[0][:, f, :]),
                                            ALU.subtract).then_inc(a_ready, 1)
                    split_lo(at.plus(2 * f + 3))
                for cb in range(NC):
                    for tb in range(NT):
                        add((NT * NC) * g + (NT * (NC + cb) + tb + 1), cb, SC[tb], tb)
                        if last and cb == NC - 1 and tb:
                            normalise(2, tb - 1)
                    if not (last and cb >= NC - 2):
                        split_lo(at.plus(2 * G + 2 + cb))

            with dve.Fori(0, GROUPS - 1) as g:
                ffn(g)
            ffn(GROUPS - 1, last=True)
            normalise(2, NT - 1)

        @block.tensor
        def _(pe):
            def products(bank, stationary, moving, tiles, first=True, last=True):
                for t in tiles:
                    for sp, mp in PASSES:
                        ins = nc.tensor.matmul(bank, stationary(sp, t), moving(mp, t),
                                               start=first and t == tiles[0] and (sp, mp) == PASSES[0],
                                               stop=last and t == tiles[-1] and (sp, mp) == PASSES[-1])
                return ins

            def turn(norm, tb):
                for q in range(4):
                    n = 4 * NT * norm + 4 * tb + q
                    wait_normalised(pe, norm, tb, q)
                    if tb:
                        pe.wait_ge(hT_done, n - 3)
                    for c in range(4):
                        ins = nc.tensor.transpose(ps[:, TP[norm][q], c * P:(c + 1) * P],
                                                  tmp[:, q, c * P:(c + 1) * P], ident[:])
                    ins.then_inc(h_turned, 1)

            ALL = slice(0, S)
            EARLY, LATE = slice(0, S // 2), slice(S // 2, S)

            def project(at, bank, tokens=ALL):
                pe.wait_ge(lo_ready, at.count(1))
                return products(ps[:, bank, tokens], lambda part, k: slab(split, at, part, k, P),
                                lambda part, k: hT[part][:, k, tokens], range(ND))

            def scores(h):
                pe.wait_ge(decay_ready, h + 1)
                pe.wait_ge(qk_done, QK * h + QK)
                for tb in range(NT):
                    t, keys = slice(tb * P, (tb + 1) * P), (tb + 1) * P
                    bank = ps[:, SC[tb], 0:keys]
                    products(bank, lambda part, d: qk[0][part][:, d, t], lambda part, d: qk[1][part][:, d, 0:keys],
                             range(NH), last=False)
                    nc.tensor.matmul(bank, decay_t[:, t], decay_h[:, 0:keys], start=False,
                                     stop=True).then_inc(s_done, 1)

            def turn_v(h):
                pe.wait_ge(v_taken, VV * h + VV)
                for b in range(2):
                    for tb in (2 * b, 2 * b + 1):
                        for d in range(NH):
                            col = (tb % 2) * HD + d * P
                            ins = nc.tensor.transpose(ps[:, PVB[b], col:col + P], vT[:, d, tb * P:(tb + 1) * P],
                                                      ident[:])
                    ins.then_inc(vt_done, 1)

            def turn_p(h):
                pe.wait_ge(p_ready, NT * h + NT)
                for b in range(PT_BANKS):
                    for s in (s for s in pt_at if pt_at[s][0] == b):
                        for tb in range(s, NT):
                            col = pt_at[s][1] + (tb - s) * P
                            ins = nc.tensor.transpose(ps[:, SC[b], col:col + P],
                                                      tmp_row(tb)[:, s * P:(s + 1) * P], ident[:])
                    ins.then_inc(pt_done, 1)

            def weigh_v(h):
                pe.wait_ge(v_ready, 2 * h + 2)
                for n, s in enumerate(pt_at):
                    b, col = pt_at[s]
                    pe.wait_ge(pt_ready, PT_BANKS * h + (b + 1))
                    for d in range(NH):
                        ins = products(ps[:, PVB[d], s * P:S], lambda part, k: v[part][:, k, d * P:(d + 1) * P],
                                       lambda part, k: pT[part][:, b * BANK + col:b * BANK + col + S - k * P],
                                       [s], first=n == 0, last=n == NT - 1)
                        if n == NT - 1:
                            ins.then_inc(pv_done, 1)

            def head(at, h, before=None):
                fresh = before is None
                if not fresh:
                    scores(before)
                    pe.wait_ge(v_taken, VV * h - 1)
                    project(at, PROJ[0]).then_inc(slab_used, 1)
                    turn_v(before)
                    project(at.plus(1), PROJ[1]).then_inc(slab_used, 1)
                    turn_p(before)
                pe.wait_ge(qk_done, QK * h + 1)
                project(at.plus(2), PROJ[0]).then_inc(slab_used, 1)
                if not fresh:
                    weigh_v(before)
                for j in range(3, PER_HEAD):
                    pe.wait_ge(qk_done, QK * h + (j - 1))
                    project(at.plus(j), PROJ[j % 2]).then_inc(slab_used, 1)

            pe.wait_ge(const_set, CONSTS)
            padded = [pad(0), pad(1)]

            def gate(tokens):
                return products(ps[:, GATE, tokens], lambda part, k: padded[part][:, k, :],
                                lambda part, k: hT[part][:, k, tokens], range(ND))

            for tb in range(NT):
                turn(0, tb)
            pe.wait_ge(hT_done, 4 * (NT // 2))
            first = At(0)
            pe.wait_ge(pad_lo, 4)
            gate(EARLY)
            project(first, PROJ[0], EARLY)
            pe.wait_ge(hT_done, 4 * NT)
            gate(LATE).then_inc(f_done, 1)
            project(first, PROJ[0], LATE).then_inc(slab_used, 1)
            project(first.plus(1), PROJ[1]).then_inc(slab_used, 1)
            head(At(0, PER_HEAD, 0), 0)
            with pe.Fori(1, H) as h:
                head(At(0, PER_HEAD, h), h, before=h - 1)

            wo = At(FIRST_WO)

            def mix(cb, tb, tiles, first=False, last=False):
                at = wo.plus(2 * cb)
                return products(ps[:, YB[cb % 2][tb], :], lambda part, k: oT[part][:, k, tb * P:(tb + 1) * P],
                                lambda part, k: slab(split, at.plus(k // 4), part, k % 4, BANK),
                                tiles, first=first, last=last)

            h = H - 1
            scores(h)
            pe.wait_ge(v_taken, VV * H)
            pe.wait_ge(lo_ready, wo.count(2))
            pe.wait_ge(o_ready, NH * h)
            early, late = range(0, NH * h), range(NH * h, NK)
            mix(0, 0, early, first=True)
            mix(0, 1, early, first=True)
            turn_v(h)
            turn_p(h)
            mix(0, 2, early, first=True)
            weigh_v(h)
            mix(0, 3, early[:4], first=True).then_inc(slab_used, 1)
            mix(0, 3, early[4:])
            pe.wait_ge(o_ready, NH * H)
            for tb in range(NT):
                ins = mix(0, tb, late, last=True)
                ins.then_inc(y_done, 1)
            for cb in range(1, NC):
                for part in range(2):
                    pe.wait_ge(lo_ready, wo.plus(2 * cb + part).count(1))
                    for tb in range(NT):
                        if part == 0 and cb >= 2:
                            pe.wait_ge(sq_done, NT + NT * (cb - 2) + tb + 1)
                        if part == 1 and cb == NC - 1 and tb == NT - 1:
                            turn(1, 0)
                        ins = mix(cb, tb, range(4 * part, 4 * part + 4), first=part == 0, last=part == 1)
                        if part == 1:
                            ins.then_inc(y_done, 1)
                    if part == 0:
                        ins.then_inc(slab_used, 1)

            def ffn(g, first=False):
                at = At(FIRST_FFN, FFN, g)
                if first:
                    turn(1, 1)
                    turn(1, 2)
                    pe.wait_ge(hT_done, 4 * NT + 4 * (NT // 2))
                    project(at, 2, EARLY)
                    turn(1, 3)
                    project(at.plus(1), 3, EARLY)
                    pe.wait_ge(hT_done, 4 * NT * 2)
                    project(at, 2, LATE).then_inc(slab_used, 1)
                    project(at.plus(1), 3, LATE).then_inc(slab_used, 1)
                for f in range(1 if first else 0, G):
                    if f >= 2:
                        pe.wait_ge(a_ready, G * g + (f - 1))
                    for up in range(2):
                        project(at.plus(2 * f + up), GU[f % 2][up]).then_inc(slab_used, 1)

                def down(cb, tb, tiles, first=True, last=True):
                    a = at.plus(2 * G + cb)
                    return products(ps[:, SC[tb], :], lambda part, k: oT[part][:, k, tb * P:(tb + 1) * P],
                                    lambda part, k: slab(split, a, part, k, BANK), tiles, first=first, last=last)

                def bank_free(cb, tb):
                    pe.wait_ge(added, (NT * NC) * g + (NT * (NC + cb - 1) + tb + 1))

                pe.wait_ge(a_ready, G * g + (G - 1))
                pe.wait_ge(lo_ready, at.plus(2 * G).count(1))
                for tb in range(2):
                    bank_free(0, tb)
                    down(0, tb, range(G - 1), last=False)
                pe.wait_ge(a_ready, G * g + G)
                for tb in range(2):
                    down(0, tb, [G - 1], first=False).then_inc(y_done, 1)
                for cb in range(NC):
                    pe.wait_ge(lo_ready, at.plus(2 * G + cb).count(1))
                    for tb in range(NT):
                        if cb or tb >= 2:
                            bank_free(cb, tb)
                            down(cb, tb, range(G)).then_inc(y_done, 1)

            ffn(0, first=True)
            with pe.Fori(1, GROUPS) as g:
                ffn(g)


_INS = ["x", "norm_mix", "fox_w_in", "fox_b_f", "fox_w_out", "norm_ffn", "ffn_w_gate_up", "ffn_w_down", "final_norm"]


def kernel(**inputs):
    import numpy as _np
    import concourse.bacc as _bacc
    from concourse import mybir as _mybir
    from concourse.bass_utils import run_bass_kernel_spmd as _run

    nc = _bacc.Bacc("TRN2", target_bir_lowering=False, num_devices=1)
    arrays, args = {}, []
    for name in _INS:
        a = _np.ascontiguousarray(inputs[name])
        arrays[f"in_{name}_dram"] = a
        args.append(nc.dram_tensor(f"in_{name}_dram", a.shape, _mybir.dt.from_np(a.dtype), kind="ExternalInput").ap())
    shape = tuple(inputs["x"].shape)
    args.append(nc.dram_tensor("out_0_dram", shape, _mybir.dt.float32, kind="ExternalOutput").ap())
    fox_layer(nc, *args)
    r = _run(nc, [arrays], core_ids=[0])
    return r.results[0]["out_0_dram"]
```

```python
from contextlib import ExitStack

import concourse.bass as bass
from concourse import mybir

F32 = mybir.dt.float32
F32R = mybir.dt.float32r
ALU = mybir.AluOpType
ACT = mybir.ActivationFunctionType
AX = mybir.AxisListType.X

P = 128
SLAB = 2048
RAW = 3
RING = 2
BANK = 512
RMS_EPS = 1e-6
FLT_MAX = 3.4028234e38
QK, VV = 4, 2
PER_HEAD = QK + VV
PASSES = ((0, 0), (0, 1), (1, 0))


class At:

    def __init__(self, off, per=0, i=0):
        assert per % (RAW * RING) == 0
        self.off, self.per, self.i = off, per, i
        self.raw, self.ring = off % RAW, off % RING

    def count(self, more=0):
        return self.per * self.i + (self.off + more)

    def landed(self):
        return (16 * (self.per // RAW)) * self.i + 16 * (self.off // RAW + 1)

    def plus(self, j):
        return At(self.off + j, self.per, self.i)


def fox_layer(nc, x, norm_mix, w_in, b_f, w_out, norm_ffn, w_gu, w_down, norm_out, out):
    _, S, D = x.shape
    H = b_f.shape[1]
    A = w_out.shape[1]
    HD = A // H
    F = w_down.shape[1]
    NT, ND = S // P, D // P
    NH = HD // P
    NK = A // P
    NC = D // BANK
    OWN = (3, 2)
    G = 4
    GROUPS = F // P // G
    FFN = 3 * G
    SCALE = HD ** -0.5
    FIRST_WO = PER_HEAD * H
    FIRST_FFN = FIRST_WO + 2 * NC
    SLABS = FIRST_FFN + FFN * GROUPS
    TRI = NT * (NT + 1) // 2 * P
    assert S == BANK and ND * P == SLAB and NC == NT == G == 4 and NH == 2 and GROUPS * G * P == F
    assert FIRST_FFN % RING == 0 and SCALE == 2.0 ** -4
    p_at = [tb * (tb + 1) // 2 * P for tb in range(NT)]
    pt_at = {0: (0, 0), 1: (1, 0), 3: (1, 3 * P), 2: (2, 0)}
    pt_cols = [BANK, BANK, 2 * P]
    PT_BANKS = len(pt_cols)

    x_v = x.rearrange("a (t p) d -> p (a t) d", p=P)
    out_v = out.rearrange("a (t p) d -> p (a t) d", p=P)
    w_in_v = w_in.rearrange("a (c p) n -> p (a c) n", p=P)
    w_out_v = w_out.rearrange("a (k p) n -> p (a k) n", p=P)
    w_gu_v = w_gu.rearrange("a (c p) n -> p (a c) n", p=P)
    w_down_v = w_down.rearrange("a (f p) n -> p (a f) n", p=P)

    with ExitStack() as ctx:
        def sb(name, shape, dt=F32):
            return ctx.enter_context(nc.sbuf_tensor(name, shape, dt))

        def sem(name):
            return ctx.enter_context(nc.semaphore(name))

        def f32(ap):
            return ap.bitcast(F32)

        hT = [sb(f"hT_{n}", [P, ND, S], F32R) for n in ("hi", "lo")]
        split = [sb(f"split_{n}", [P, RING, SLAB], F32R) for n in ("hi", "lo")]
        raw = sb("raw", [P, RAW, SLAB])
        oT = [sb(f"oT_{n}", [P, NK, S], F32R) for n in ("hi", "lo")]
        tmp = sb("tmp", [P, 4, BANK])
        ident = sb("ident", [P, P])
        bound = sb("bound", [P, P])
        with nc.sbuf_tensor("xres", [P, NT, D], F32) as xres, nc.sbuf_tensor("gain", [P, D], F32) as gain:
            pass
        qk = [[sb(f"{w}T_{n}", [P, NH, S], F32R) for n in ("hi", "lo")] for w in "qk"]
        v = [sb(f"v_{n}", [P, NT, HD], F32R) for n in ("hi", "lo")]
        pT = [sb(f"pT_{n}", [P, TRI], F32R) for n in ("hi", "lo")]
        vT = sb("vT", [P, NH, S])
        decay_t = sb("decay_t", [P, S], F32R)
        decay_s = sb("decay_s", [P, S], F32R)
        decay_h = sb("decay_h", [P, S], F32R)
        rows = sb("rows", [P, H, 4])
        row_of = sb("row_of", [P, 8])
        head_of = sb("head_of", [P, H])
        wf = sb("wf", [P, ND, H])
        bf_all = sb("bf_all", [P, H])
        bf = sb("bf", [P, 1])
        half = sb("half", [P, 1])
        sumsq = sb("sumsq", [P, NT, NC])
        pairs = sb("pairs", [P, 2])
        var = sb("var", [P, NT])
        rstd = sb("rstd", [P, NT])
        negmax = sb("negmax", [P, NT])
        rowsum = sb("rowsum", [P, NT])
        rinv = sb("rinv", [P, NT])
        warm = f32(decay_s[:])

        ps = ctx.enter_context(nc.psum_tensor("ps", [P, 8, BANK], F32))
        PROJ = (0, 1)
        PVB = (2, 3)
        GATE = PVB[0]
        SC = (4, 5, 6, 7)
        YB = ((0, 1, 7, 4), (2, 3, 5, 6))
        GU = ((2, 3), (0, 1))

        x_in = [sem(f"x_in{i}") for i in range(NT)]
        gain_in = sem("gain_in")
        wf_in = sem("wf_in")
        bf_in = sem("bf_in")
        raw_in = [sem(f"raw_in{i}") for i in range(RAW)]
        out_done = sem("out_done")
        hi_ready = sem("hi_ready")
        lo_ready = sem("lo_ready")
        slab_used = sem("slab_used")
        const_set = sem("const_set")
        sq_done = sem("sq_done")
        stat = sem("stat")
        var_step = sem("var_step")
        rstd_ready = sem("rstd_ready")
        h_ready = sem("h_ready")
        scaled = sem("scaled")
        h_pool = sem("h_pool")
        weighted = sem("weighted")
        out_act = sem("out_act")
        out_dve = sem("out_dve")
        h_turned = sem("h_turned")
        hT_hi = sem("hT_hi")
        hT_done = sem("hT_done")
        pad_hi = sem("pad_hi")
        pad_lo = sem("pad_lo")
        warmed = sem("warmed")
        f_done = sem("f_done")
        gate_v = sem("gate_v")
        gate_s = sem("gate_s")
        qk_hi = sem("qk_hi")
        qk_done = sem("qk_done")
        v_taken = sem("v_taken")
        decay_ready = sem("decay_ready")
        s_done = sem("s_done")
        masked = sem("masked")
        max_ready = sem("max_ready")
        exp_done = sem("exp_done")
        inv_ready = sem("inv_ready")
        p_ready = sem("p_ready")
        vt_done = sem("vt_done")
        v_hi = sem("v_hi")
        v_ready = sem("v_ready")
        pt_done = sem("pt_done")
        pt_hi = sem("pt_hi")
        pt_ready = sem("pt_ready")
        pv_done = sem("pv_done")
        o_hi = sem("o_hi")
        o_ready = sem("o_ready")
        y_done = sem("y_done")
        added = sem("added")
        silu_done = sem("silu_done")
        a_done = sem("a_done")
        a_hi = sem("a_hi")
        a_ready = sem("a_ready")

        block = ctx.enter_context(nc.Block())

        def tmp_row(tb):
            return tmp[:, :, :].rearrange("p a b -> p (a b)")[:, p_at[tb]:p_at[tb] + (tb + 1) * P]

        def pad(part):
            return oT[0][:, part * 4:(part + 1) * 4, :].rearrange("p a b -> p (a b)").rearrange(
                "p (k n) -> p k n", n=P)

        def own_chunks(norm, tb, q):
            return NT * sum(OWN[:norm]) + OWN[norm] * tb + q + 1

        def shared_chunks(norm, tb, q):
            return NT * (norm * NC - sum(OWN[:norm])) + (NC - OWN[norm]) * tb + q - OWN[norm] + 1

        def wait_normalised(eng, norm, tb, q):
            if q < OWN[norm]:
                eng.wait_ge(h_ready, own_chunks(norm, tb, q))
            else:
                eng.wait_ge(h_pool, shared_chunks(norm, tb, q))

        DOWN = [(cb, tb) for cb in range(NC) for tb in range(NT)]
        LAST_DOWN = DOWN[:NT * (NC - 2)] + [(2, 0), (2, 1), (3, 0), (3, 1), (2, 2), (3, 2), (2, 3), (3, 3)]

        def nth(cb, tb, last=True):
            return (LAST_DOWN if last else DOWN).index((cb, tb)) + 1

        def down_bank(cb, tb, last):
            return (PROJ + PVB)[tb] if last and cb == NC - 1 else SC[tb]

        def finish_before(cb, tb, finish):
            at = LAST_DOWN.index((cb, tb))
            if at and LAST_DOWN[at - 1][0] == NC - 1:
                finish(LAST_DOWN[at - 1][1])
            if at == len(LAST_DOWN) - 1:
                finish(tb)

        def squared(cb, tb):
            return NT + NT * NC + nth(cb, tb)

        def weighed(cb, tb):
            return [at for at in LAST_DOWN if at[0] < NC - 1].index((cb, tb)) + 1

        def y(tb, cb):
            return xres[:, tb, cb * BANK:(cb + 1) * BANK]

        def turned(norm, tb, q):
            if norm == 0 and tb == 1:
                return (PROJ + PVB)[q], 0
            before = tb - 1 if norm or tb != 2 else 0
            return (YB[0] if norm else SC)[q], NT * NC * norm + NC * before + q + 1 if tb else 0

        def wait_used(eng, at):
            n = at.off
            if n < FIRST_WO:
                eng.wait_ge(slab_used, at.per * at.i + (n + 1))
            elif n < FIRST_FFN:
                cb, second = divmod(n - FIRST_WO, 2)
                if second:
                    eng.wait_ge(y_done, NT * (cb + 1))
                else:
                    eng.wait_ge(slab_used, FIRST_WO + cb + 1)
            else:
                j = n - FIRST_FFN
                if j < 2 * G:
                    eng.wait_ge(slab_used, (2 * G) * at.i + (FIRST_WO + NC + j + 1))
                else:
                    eng.wait_ge(y_done, (NT * NC) * at.i + (NT * NC + NT * (j - 2 * G + 1)))

        def slab(parts, at, part, tile, cols):
            return parts[part][:, at.ring, tile * cols:(tile + 1) * cols]

        @block.sync
        def _(sp):
            def load(at, view, source, first=False):
                if not first:
                    sp.wait_ge(lo_ready, at.count(1 - RAW))
                sp.dma_start(view, source).then_inc(raw_in[at.raw], 16)

            def tile_of(at, cols):
                return raw[:, at.raw, :].rearrange("p (k n) -> p k n", n=cols)

            def load_head(h):
                at = At(0, PER_HEAD, h)
                for j in range(PER_HEAD):
                    a = at.plus(j)
                    col = h * HD + ((j // NH) * A + (j % NH) * P)
                    load(a, tile_of(a, P), w_in_v[:, :, bass.ds(col, P)],
                         first=isinstance(h, int) and j < RAW)

            for tb in range(NT):
                sp.dma_start(xres[:, tb, :], x_v[:, tb, :]).then_inc(x_in[tb], 16)
                if tb == 0:
                    sp.dma_start(gain[:], norm_mix.rearrange("a d -> (a d)").partition_broadcast(P)
                                 ).then_inc(gain_in, 16)
                if tb == 1:
                    with nc.allow_non_contiguous_dma(reason="the gate's four columns"):
                        sp.dma_start(wf[:], w_in_v[:, :, 3 * A:3 * A + H]).then_inc(wf_in, 16)
            sp.dma_start(bf_all[:], b_f.rearrange("a h -> (a h)").partition_broadcast(P)).then_inc(bf_in, 16)
            load_head(0)
            with sp.Fori(1, H) as h:
                load_head(h)
            for j in range(2 * NC):
                a = At(FIRST_WO + j)
                cb, kt = j // 2, (j % 2) * (NK // 2)
                load(a, tile_of(a, BANK), w_out_v[:, kt:kt + NK // 2, cb * BANK:(cb + 1) * BANK])
            with sp.Fori(0, GROUPS) as g:
                at = At(FIRST_FFN, FFN, g)
                for j in range(2 * G):
                    a = at.plus(j)
                    load(a, tile_of(a, P), w_gu_v[:, :, bass.ds(g * (G * P) + ((j // 2) * P + (j % 2) * F), P)])
                for cb in range(NC):
                    a = at.plus(2 * G + cb)
                    load(a, tile_of(a, BANK), w_down_v[:, bass.ds(g * G, G), cb * BANK:(cb + 1) * BANK])
            for tb in range(NT):
                for q, ready, count in ((1, out_act, 1), (3, out_dve, 1), (0, out_dve, 2), (2, out_act, 2)):
                    sp.wait_ge(ready, 2 * tb + count)
                    sp.dma_start(out_v[:, tb, q * BANK:(q + 1) * BANK], y(tb, q)).then_inc(out_done, 16)
            sp.wait_ge(out_done, 16 * NT * NC)

        @block.gpsimd
        def _(pool):
            nc.gpsimd.memset(warm, 0.0).then_inc(const_set, 1)
            nc.gpsimd.memset(half[:], -0.5).then_inc(const_set, 1)
            nc.gpsimd.memset(ident[:], 0.0).then_inc(const_set, 1)
            nc.gpsimd.memset(bound[:], FLT_MAX).then_inc(const_set, 1)
            nc.gpsimd.memset(rows[:], 0.0).then_inc(const_set, 1)
            pool.wait_ge(const_set, 5)
            nc.gpsimd.affine_select(out=ident[:], in_=ident[:], compare_op=ALU.not_equal, fill=1.0, base=0,
                                    pattern=[[-1, P]], channel_multiplier=1).then_inc(const_set, 1)
            for part in range(2):
                nc.gpsimd.memset(oT[0][:, part * 4:(part + 1) * 4, :].bitcast(F32), 0.0).then_inc(const_set, 1)
            nc.gpsimd.affine_select(out=bound[:], in_=bound[:], compare_op=ALU.is_ge, fill=-FLT_MAX, base=0,
                                    pattern=[[-1, P]], channel_multiplier=1).then_inc(const_set, 1)
            nc.gpsimd.affine_select(out=rows[:], in_=rows[:], compare_op=ALU.not_equal, fill=1.0, base=0,
                                    pattern=[[-32, H], [-1, 4]], channel_multiplier=1).then_inc(const_set, 1)
            steps = 0

            def step(ins):
                nonlocal steps
                steps += 1
                ins.then_inc(var_step, 1)
                pool.wait_ge(var_step, steps)

            for norm in range(2):
                for tb in range(NT):
                    v1 = var[:, tb:tb + 1]
                    if norm == 0:
                        pool.wait_ge(sq_done, tb + 1)
                        total = sumsq[:, tb, 0:1]
                    else:
                        pool.wait_ge(sq_done, NT + NT * NC * norm - NT + tb + 1)
                        step(nc.gpsimd.tensor_tensor(out=pairs[:], in0=sumsq[:, tb, 0:2], in1=sumsq[:, tb, 2:4],
                                                     op=ALU.add))
                        step(nc.gpsimd.tensor_tensor(out=v1, in0=pairs[:, 0:1], in1=pairs[:, 1:2], op=ALU.add))
                        total = v1
                    step(nc.gpsimd.tensor_scalar(v1, total, 1.0 / D, RMS_EPS, ALU.mult, ALU.add))
                    nc.gpsimd.tensor_tensor(out=rstd[:, tb:tb + 1], in0=v1, in1=half[:],
                                            op=ALU.pow).then_inc(rstd_ready, 1)
                    if tb == 0:
                        pool.wait_ge(gain_in, 16 * (norm + 1))
                    for q in range(OWN[norm], NC):
                        pool.wait_ge(scaled, shared_chunks(norm, tb, q))
                        nc.gpsimd.tensor_tensor(out=tmp[:, q, :], in0=tmp[:, q, :],
                                                in1=gain[:, q * BANK:(q + 1) * BANK],
                                                op=ALU.mult).then_inc(h_pool, 1)
            pool.wait_ge(gain_in, 16 * 3)
            for cb, tb in LAST_DOWN:
                v1 = var[:, tb:tb + 1]
                pool.wait_ge(sq_done, squared(cb, tb))
                if cb < NC - 1:
                    nc.gpsimd.tensor_tensor(out=y(tb, cb), in0=y(tb, cb), in1=gain[:, cb * BANK:(cb + 1) * BANK],
                                            op=ALU.mult).then_inc(weighted, 1)
                if cb == NC - 2:
                    step(nc.gpsimd.tensor_tensor(out=v1, in0=sumsq[:, tb, 0:1], in1=sumsq[:, tb, 1:2], op=ALU.add))
                    step(nc.gpsimd.tensor_tensor(out=v1, in0=v1, in1=sumsq[:, tb, 2:3], op=ALU.add))
                    step(nc.gpsimd.tensor_scalar(v1, v1, 1.0 / D, RMS_EPS, ALU.mult, ALU.add))
                if cb == NC - 1:
                    step(nc.gpsimd.tensor_scalar(v1, sumsq[:, tb, 3:4], 1.0 / D, v1, ALU.mult, ALU.add))
                    nc.gpsimd.tensor_tensor(out=rstd[:, tb:tb + 1], in0=v1, in1=half[:],
                                            op=ALU.pow).then_inc(rstd_ready, 1)

        CONSTS = 10

        @block.scalar
        def _(act):
            def split_hi(at, first=False):
                act.wait_ge(raw_in[at.raw], at.landed())
                if not first:
                    wait_used(act, at.plus(-RING))
                nc.scalar.activation(split[0][:, at.ring, :], raw[:, at.raw, :], ACT.Copy).then_inc(hi_ready, 1)

            def take_hT(norm, tb, chunks=range(NC)):
                for q in chunks:
                    act.wait_ge(h_turned, 4 * NT * norm + 4 * tb + q + 1)
                    nc.scalar.activation(hT[0][:, 4 * q:4 * q + 4, tb * P:(tb + 1) * P],
                                         ps[:, turned(norm, tb, q)[0], :].rearrange("p (c t) -> p c t", t=P),
                                         ACT.Copy).then_inc(hT_hi, 1)

            def scale(norm, tb):
                act.wait_ge(rstd_ready, NT * norm + tb + 1)
                for q in range(OWN[norm], NC):
                    if tb:
                        act.wait_ge(h_turned, 4 * NT * norm + 4 * tb + q - 3)
                    nc.scalar.activation(tmp[:, q, :], y(tb, q), ACT.Copy,
                                         scale=rstd[:, tb:tb + 1]).then_inc(scaled, 1)

            def softmax(h):
                for tb in range(NT):
                    act.wait_ge(max_ready, NT * h + (tb + 1))
                    nc.scalar.activation(tmp_row(tb), ps[:, SC[tb], 0:(tb + 1) * P], ACT.Exp,
                                         bias=negmax[:, tb:tb + 1],
                                         accum_out=rowsum[:, tb:tb + 1]).then_inc(exp_done, 1)

            def take_v(h):
                for b in range(2):
                    act.wait_ge(vt_done, 2 * h + (b + 1))
                    nc.scalar.activation(v[0][:, 2 * b:2 * b + 2, :],
                                         ps[:, PVB[b], :].rearrange("p (t d) -> p t d", d=HD),
                                         ACT.Copy).then_inc(v_hi, 1)

            def take_pT(h):
                for b in range(PT_BANKS):
                    act.wait_ge(pt_done, PT_BANKS * h + (b + 1))
                    nc.scalar.activation(pT[0][:, b * BANK:b * BANK + pt_cols[b]], ps[:, SC[b], 0:pt_cols[b]],
                                         ACT.Copy).then_inc(pt_hi, 1)

            def take_o(h):
                for d in range(NH):
                    act.wait_ge(pv_done, NH * h + (d + 1))
                    nc.scalar.activation(oT[0][:, h * NH + d, :], ps[:, PVB[d], :], ACT.Copy).then_inc(o_hi, 1)

            def take_qk(h, at, j):
                wait_used(act, at.plus(j))
                nc.scalar.activation(qk[j // NH][0][:, j % NH, :], ps[:, PROJ[j % 2], :], ACT.Copy,
                                     scale=SCALE if j < NH else 1.0).then_inc(qk_hi, 1)

            def head(at, h, before=None):
                fresh = before is None
                if not fresh:
                    split_hi(at.plus(1))
                    softmax(before)
                take_qk(h, at, 0)
                split_hi(at.plus(2))
                if not fresh:
                    take_v(before)
                take_qk(h, at, 1)
                split_hi(at.plus(3))
                if not fresh:
                    take_pT(before)
                take_qk(h, at, 2)
                split_hi(at.plus(4))
                if not fresh:
                    take_o(before)
                take_qk(h, at, 3)
                split_hi(at.plus(5))
                for j in range(VV):
                    wait_used(act, at.plus(QK + j))
                    nc.scalar.activation(vT[:, j, :], ps[:, PROJ[j % 2], :], ACT.Copy).then_inc(v_taken, 1)
                    if j == 0:
                        split_hi(at.plus(6))

            def square_x(tb):
                act.wait_ge(x_in[tb], 16)
                if tb >= 2:
                    act.wait_ge(sq_done, tb - 1)
                nc.scalar.activation(oT[1][:, NC * (tb % 2):NC * (tb % 2) + NC, :],
                                     xres[:, tb, :].rearrange("p (c n) -> p c n", n=BANK),
                                     ACT.Square, accum_out=sumsq[:, tb, 0:1]).then_inc(sq_done, 1)

            square_x(0)
            scale(0, 0)
            take_hT(0, 0, range(0, NC // 2))
            square_x(1)
            take_hT(0, 0, range(NC // 2, NC))
            act.wait_ge(wf_in, 16)
            act.wait_ge(const_set, CONSTS)
            for r in range(4):
                nc.scalar.activation(pad(0)[:, :, r::32], wf[:], ACT.Copy).then_inc(pad_hi, 1)
            scale(0, 1)
            take_hT(0, 1)
            square_x(2)
            square_x(3)
            scale(0, 2)
            split_hi(At(0), first=True)
            take_hT(0, 2)
            scale(0, 3)
            take_hT(0, 3)
            split_hi(At(1), first=True)
            act.wait_ge(gate_v, 1)
            nc.scalar.activation(tmp[:, 1, :], tmp[:, 0, :], ACT.Abs).then_inc(gate_s, 1)
            act.wait_ge(gate_s, 1)
            nc.scalar.activation(tmp[:, 2, :], tmp[:, 1, :], ACT.Exp, scale=-1.0).then_inc(gate_s, 1)
            act.wait_ge(gate_s, 2)
            nc.scalar.activation(tmp[:, 3, :], tmp[:, 2, :], ACT.Ln, bias=1.0).then_inc(gate_s, 1)
            head(At(0, PER_HEAD, 0), 0)
            with act.Fori(1, H) as h:
                head(At(0, PER_HEAD, h), h, before=h - 1)
            wo = At(FIRST_WO)
            split_hi(wo.plus(1))
            softmax(H - 1)
            take_v(H - 1)
            take_pT(H - 1)
            take_o(H - 1)
            act.wait_ge(pv_done, NH * H)
            act.wait_ge(pt_ready, PT_BANKS * H)
            for cb in range(NC):
                act.dma_start(xres[:, :, cb * BANK:(cb + 1) * BANK],
                              x_v[:, :, cb * BANK:(cb + 1) * BANK]).then_inc(x_in[cb], 16)
            act.dma_start(gain[:], norm_ffn.rearrange("a d -> (a d)").partition_broadcast(P)).then_inc(gain_in, 16)

            def square(count, cb, tb, scratch):
                act.wait_ge(added, count)
                nc.scalar.activation(scratch, y(tb, cb),
                                     ACT.Square, accum_out=sumsq[:, tb, cb:cb + 1]).then_inc(sq_done, 1)

            split_hi(wo.plus(2))
            for cb in range(NC - 1):
                for tb in range(NT):
                    square(NT * cb + tb + 1, cb, tb, ps[:, YB[cb % 2][tb], :])
                split_hi(wo.plus(2 * cb + 3))
                if cb < NC - 2:
                    split_hi(wo.plus(2 * cb + 4))
            last = NC - 1
            for tb in range(NT):
                if tb == NT - 1:
                    split_hi(wo.plus(2 * NC))
                square(NT * last + tb + 1, last, tb, ps[:, YB[last % 2][tb], :])
                if tb == NT - 1:
                    split_hi(wo.plus(2 * NC + 1))
                    scale(1, tb)
                if tb:
                    take_hT(1, tb - 1)
                if tb < NT - 1:
                    scale(1, tb)
            take_hT(1, NT - 1)
            wait_normalised(act, 1, NT - 1, OWN[1] - 1)
            wait_normalised(act, 1, NT - 1, NC - 1)
            act.dma_start(gain[:], norm_out.partition_broadcast(P)).then_inc(gain_in, 16)

            def finish(tb):
                act.wait_ge(rstd_ready, NT * 2 + tb + 1)
                for cb in (1, 2):
                    act.wait_ge(weighted, weighed(cb, tb))
                    nc.scalar.activation(y(tb, cb), y(tb, cb), ACT.Copy,
                                         scale=rstd[:, tb:tb + 1]).then_inc(out_act, 1)

            def ffn(g, last=False):
                at = At(FIRST_FFN, FFN, g)
                for f in range(G):
                    wait_used(act, at.plus(2 * f))
                    nc.scalar.activation(tmp[:, f % 2, :], ps[:, GU[f % 2][0], :], ACT.Silu).then_inc(silu_done, 1)
                    split_hi(at.plus(2 * f + 2))
                    act.wait_ge(a_done, G * g + (f + 1))
                    nc.scalar.activation(oT[0][:, f, :], tmp[:, 2 + f % 2, :], ACT.Copy).then_inc(a_hi, 1)
                    split_hi(at.plus(2 * f + 3))
                if not last:
                    for cb in range(NC):
                        split_hi(at.plus(2 * G + 2 + cb))
                    return
                for cb, tb in LAST_DOWN:
                    if cb < NC - 2 and tb == 0:
                        split_hi(at.plus(2 * G + 2 + cb))
                    if cb:
                        act.wait_ge(sq_done, squared(cb - 1, tb))
                    square(NT * NC * GROUPS + nth(cb, tb), cb, tb, tmp[:, tb, :])
                    finish_before(cb, tb, finish)

            with act.Fori(0, GROUPS - 1) as g:
                ffn(g)
            ffn(GROUPS - 1, last=True)

        @block.vector
        def _(dve):
            def split_lo(at):
                dve.wait_ge(hi_ready, at.count(1))
                nc.vector.tensor_tensor(split[1][:, at.ring, :], raw[:, at.raw, :],
                                        f32(split[0][:, at.ring, :]), ALU.subtract).then_inc(lo_ready, 1)

            def take_hT(norm, tb):
                for q in range(4):
                    n = 4 * NT * norm + 4 * tb + q
                    dve.wait_ge(hT_hi, n + 1)
                    nc.vector.tensor_tensor(hT[1][:, 4 * q:4 * q + 4, tb * P:(tb + 1) * P],
                                            ps[:, turned(norm, tb, q)[0], :].rearrange("p (c t) -> p c t", t=P),
                                            f32(hT[0][:, 4 * q:4 * q + 4, tb * P:(tb + 1) * P]),
                                            ALU.subtract).then_inc(hT_done, 1)

            def normalise(norm, tb):
                dve.wait_ge(rstd_ready, NT * norm + tb + 1)
                if tb == 0:
                    dve.wait_ge(gain_in, 16 * (norm + 1))
                for q in range(OWN[norm]):
                    if tb:
                        dve.wait_ge(h_turned, 4 * NT * norm + 4 * tb + q - 3)
                    nc.vector.scalar_tensor_tensor(tmp[:, q, :], y(tb, q),
                                                   rstd[:, tb:tb + 1], gain[:, q * BANK:(q + 1) * BANK],
                                                   ALU.mult, ALU.mult).then_inc(h_ready, 1)

            def softmax(h):
                for tb in range(NT):
                    dve.wait_ge(s_done, NT * h + (tb + 1))
                    diag = ps[:, SC[tb], tb * P:(tb + 1) * P]
                    nc.vector.tensor_tensor(diag, diag, bound[:], ALU.min).then_inc(masked, 1)
                    dve.wait_ge(masked, NT * h + (tb + 1))
                    nc.vector.reduce_max(negmax[:, tb:tb + 1], ps[:, SC[tb], 0:(tb + 1) * P], AX,
                                         negate=True).then_inc(max_ready, 1)
                for tb in range(NT):
                    dve.wait_ge(exp_done, NT * h + (tb + 1))
                    nc.vector.reciprocal(rinv[:, tb:tb + 1], rowsum[:, tb:tb + 1]).then_inc(inv_ready, 1)
                    dve.wait_ge(inv_ready, NT * h + (tb + 1))
                    nc.vector.tensor_scalar(tmp_row(tb), tmp_row(tb), rinv[:, tb:tb + 1], None,
                                            ALU.mult).then_inc(p_ready, 1)

            def take_v(h):
                for b in range(2):
                    dve.wait_ge(v_hi, 2 * h + (b + 1))
                    nc.vector.tensor_tensor(v[1][:, 2 * b:2 * b + 2, :],
                                            ps[:, PVB[b], :].rearrange("p (t d) -> p t d", d=HD),
                                            f32(v[0][:, 2 * b:2 * b + 2, :]), ALU.subtract).then_inc(v_ready, 1)

            def take_pT(h):
                for b in range(PT_BANKS):
                    at = slice(b * BANK, b * BANK + pt_cols[b])
                    dve.wait_ge(pt_hi, PT_BANKS * h + (b + 1))
                    nc.vector.tensor_tensor(pT[1][:, at], ps[:, SC[b], 0:pt_cols[b]], f32(pT[0][:, at]),
                                            ALU.subtract).then_inc(pt_ready, 1)

            def take_o(h):
                for d in range(NH):
                    dve.wait_ge(o_hi, NH * h + (d + 1))
                    nc.vector.tensor_tensor(oT[1][:, h * NH + d, :], ps[:, PVB[d], :],
                                            f32(oT[0][:, h * NH + d, :]), ALU.subtract).then_inc(o_ready, 1)

            def take_qk(h, j):
                dve.wait_ge(qk_hi, QK * h + (j + 1))
                hi, lo = (part[:, j % NH, :] for part in qk[j // NH])
                nc.vector.scalar_tensor_tensor(lo, ps[:, PROJ[j % 2], :], SCALE if j < NH else 1.0, f32(hi),
                                               ALU.mult, ALU.subtract).then_inc(qk_done, 1)

            def head(at, h, head_col, before=None):
                fresh = before is None
                if not fresh:
                    split_lo(at.plus(1))
                    softmax(before)
                take_qk(h, 0)
                nc.vector.tensor_scalar(decay_h[:], f32(decay_s[:]), head_col, None,
                                        ALU.mult).then_inc(decay_ready, 1)
                split_lo(at.plus(2))
                if not fresh:
                    take_v(before)
                take_qk(h, 1)
                split_lo(at.plus(3))
                if not fresh:
                    take_pT(before)
                take_qk(h, 2)
                split_lo(at.plus(4))
                if not fresh:
                    take_o(before)
                take_qk(h, 3)
                split_lo(at.plus(5))
                split_lo(at.plus(6))

            normalise(0, 0)
            take_hT(0, 0)
            normalise(0, 1)
            for r in range(4):
                dve.wait_ge(pad_hi, r + 1)
                nc.vector.tensor_tensor(pad(1)[:, :, r::32], wf[:], f32(pad(0)[:, :, r::32]),
                                        ALU.subtract).then_inc(pad_lo, 1)
            take_hT(0, 1)
            normalise(0, 2)
            split_lo(At(0))
            take_hT(0, 2)
            normalise(0, 3)
            take_hT(0, 3)
            split_lo(At(1))
            nc.vector.reduce_sum(head_of[:], rows[:], AX).then_inc(stat, 1)
            nc.vector.reduce_sum(row_of[:, 0:4], rows[:].rearrange("p h r -> p r h"), AX).then_inc(stat, 1)
            dve.wait_ge(stat, 2)
            nc.vector.tensor_scalar(row_of[:, 6:8], row_of[:, 2:4], -1.0, None, ALU.mult).then_inc(stat, 1)
            nc.vector.tensor_tensor(row_of[:, 4:5], row_of[:, 0:1], row_of[:, 1:2], ALU.add).then_inc(stat, 1)
            nc.vector.tensor_tensor(row_of[:, 5:6], row_of[:, 2:3], row_of[:, 3:4], ALU.add).then_inc(stat, 1)
            z, soft, logs, cum, mixed = tmp[:, 0, :], tmp[:, 3, :], tmp[:, 1, :], tmp[:, 2, :], tmp[:, 3, :]
            dve.wait_ge(bf_in, 16)
            nc.vector.tensor_tensor(bf_all[:], bf_all[:], head_of[:], ALU.mult).then_inc(stat, 1)
            dve.wait_ge(stat, 6)
            nc.vector.reduce_sum(bf[:], bf_all[:], AX).then_inc(stat, 1)
            dve.wait_ge(stat, 7)
            dve.wait_ge(f_done, 1)
            nc.vector.tensor_scalar(z, ps[:, GATE, :], bf[:, 0:1], None, ALU.add).then_inc(gate_v, 1)
            dve.wait_ge(gate_s, 3)
            nc.vector.scalar_tensor_tensor(logs, z, 0.0, soft, ALU.min, ALU.subtract).then_inc(gate_v, 1)
            dve.wait_ge(gate_v, 2)
            nc.vector.memset(z, 1.0).then_inc(gate_v, 1)
            dve.wait_ge(gate_v, 3)
            nc.vector.tensor_tensor_scan(cum, z, logs, 0.0, ALU.mult, ALU.add).then_inc(gate_v, 1)
            dve.wait_ge(gate_v, 4)
            nc.vector.tensor_copy(decay_h[:], cum).then_inc(gate_v, 1)
            dve.wait_ge(gate_v, 5)
            nc.vector.tensor_tensor(logs, cum, f32(decay_h[:]), ALU.subtract).then_inc(gate_v, 1)
            dve.wait_ge(stat, 5)
            nc.vector.tensor_scalar(mixed, f32(decay_h[:]), row_of[:, 0:1], row_of[:, 5:6], ALU.mult,
                                    ALU.add).then_inc(gate_v, 1)
            nc.vector.tensor_scalar(z, f32(decay_h[:]), row_of[:, 6:7], row_of[:, 4:5], ALU.mult,
                                    ALU.add).then_inc(gate_v, 1)
            dve.wait_ge(gate_v, 8)
            nc.vector.scalar_tensor_tensor(decay_t[:], logs, row_of[:, 1:2], mixed, ALU.mult,
                                           ALU.add).then_inc(gate_v, 1)
            nc.vector.scalar_tensor_tensor(decay_s[:], logs, row_of[:, 7:8], z, ALU.mult,
                                           ALU.add).then_inc(gate_v, 1)
            dve.wait_ge(gate_v, 10)
            head(At(0, PER_HEAD, 0), 0, head_of[:, 0:1])
            with dve.Fori(1, H) as h:
                head(At(0, PER_HEAD, h), h, head_of[:, bass.ds(h, 1)], before=h - 1)
            wo = At(FIRST_WO)
            split_lo(wo.plus(1))
            softmax(H - 1)
            take_v(H - 1)
            take_pT(H - 1)
            take_o(H - 1)

            def add(count, cb, bank, tb):
                dve.wait_ge(y_done, count)
                part = y(tb, cb)
                nc.vector.tensor_tensor(part, ps[:, bank, :], part, ALU.add).then_inc(added, 1)

            split_lo(wo.plus(2))
            for cb in range(NC - 1):
                dve.wait_ge(x_in[cb], 32)
                for tb in range(NT):
                    add(NT * cb + tb + 1, cb, YB[cb % 2][tb], tb)
                split_lo(wo.plus(2 * cb + 3))
                if cb < NC - 2:
                    split_lo(wo.plus(2 * cb + 4))
            cb = NC - 1
            dve.wait_ge(x_in[cb], 32)
            for tb in range(NT):
                if tb == NT - 1:
                    split_lo(wo.plus(2 * NC))
                add(NT * cb + tb + 1, cb, YB[cb % 2][tb], tb)
                if tb == NT - 1:
                    split_lo(wo.plus(2 * NC + 1))
                    normalise(1, tb)
                if tb:
                    take_hT(1, tb - 1)
                if tb < NT - 1:
                    normalise(1, tb)
            take_hT(1, NT - 1)

            def finish(tb):
                dve.wait_ge(rstd_ready, NT * 2 + tb + 1)
                dve.wait_ge(gain_in, 16 * 3)
                nc.vector.scalar_tensor_tensor(y(tb, NC - 1), y(tb, NC - 1), rstd[:, tb:tb + 1],
                                               gain[:, (NC - 1) * BANK:NC * BANK],
                                               ALU.mult, ALU.mult).then_inc(out_dve, 1)
                dve.wait_ge(weighted, tb + 1)
                nc.vector.tensor_scalar(y(tb, 0), y(tb, 0), rstd[:, tb:tb + 1], None,
                                        ALU.mult).then_inc(out_dve, 1)

            def ffn(g, last=False):
                at = At(FIRST_FFN, FFN, g)
                for f in range(G):
                    split_lo(at.plus(2 * f + 2))
                    dve.wait_ge(silu_done, G * g + (f + 1))
                    wait_used(dve, at.plus(2 * f + 1))
                    a = tmp[:, 2 + f % 2, :]
                    nc.vector.tensor_tensor(a, ps[:, GU[f % 2][1], :], tmp[:, f % 2, :],
                                            ALU.mult).then_inc(a_done, 1)
                    dve.wait_ge(a_hi, G * g + (f + 1))
                    nc.vector.tensor_tensor(oT[1][:, f, :], a, f32(oT[0][:, f, :]),
                                            ALU.subtract).then_inc(a_ready, 1)
                    split_lo(at.plus(2 * f + 3))
                for cb, tb in LAST_DOWN if last else DOWN:
                    add((NT * NC) * g + (NT * NC + nth(cb, tb, last)), cb, down_bank(cb, tb, last), tb)
                    if last:
                        finish_before(cb, tb, finish)
                    if tb == NT - 1 and not (last and cb >= NC - 2):
                        split_lo(at.plus(2 * G + 2 + cb))

            with dve.Fori(0, GROUPS - 1) as g:
                ffn(g)
            ffn(GROUPS - 1, last=True)

        @block.tensor
        def _(pe):
            def products(bank, stationary, moving, tiles, first=True, last=True):
                for t in tiles:
                    for sp, mp in PASSES:
                        ins = nc.tensor.matmul(bank, stationary(sp, t), moving(mp, t),
                                               start=first and t == tiles[0] and (sp, mp) == PASSES[0],
                                               stop=last and t == tiles[-1] and (sp, mp) == PASSES[-1])
                return ins

            def turn(norm, tb):
                for q in range(4):
                    bank, used = turned(norm, tb, q)
                    wait_normalised(pe, norm, tb, q)
                    if used:
                        pe.wait_ge(hT_done, used)
                    for c in range(4):
                        ins = nc.tensor.transpose(ps[:, bank, c * P:(c + 1) * P],
                                                  tmp[:, q, c * P:(c + 1) * P], ident[:])
                    ins.then_inc(h_turned, 1)

            ALL = slice(0, S)
            EARLY, LATE = slice(0, S // 2), slice(S // 2, S)

            def project(at, bank, tokens=ALL, tiles=range(ND)):
                pe.wait_ge(lo_ready, at.count(1))
                return products(ps[:, bank, tokens], lambda part, k: slab(split, at, part, k, P),
                                lambda part, k: hT[part][:, k, tokens], tiles, first=tiles[0] == 0,
                                last=tiles[-1] == ND - 1)

            def scores(h):
                pe.wait_ge(decay_ready, h + 1)
                pe.wait_ge(qk_done, QK * h + QK)
                for tb in range(NT):
                    t, keys = slice(tb * P, (tb + 1) * P), (tb + 1) * P
                    bank = ps[:, SC[tb], 0:keys]
                    products(bank, lambda part, d: qk[0][part][:, d, t], lambda part, d: qk[1][part][:, d, 0:keys],
                             range(NH), last=False)
                    nc.tensor.matmul(bank, decay_t[:, t], decay_h[:, 0:keys], start=False,
                                     stop=True).then_inc(s_done, 1)

            def turn_v(h):
                pe.wait_ge(v_taken, VV * h + VV)
                for b in range(2):
                    for tb in (2 * b, 2 * b + 1):
                        for d in range(NH):
                            col = (tb % 2) * HD + d * P
                            ins = nc.tensor.transpose(ps[:, PVB[b], col:col + P], vT[:, d, tb * P:(tb + 1) * P],
                                                      ident[:])
                    ins.then_inc(vt_done, 1)

            def turn_p(h):
                pe.wait_ge(p_ready, NT * h + NT)
                for b in range(PT_BANKS):
                    for s in (s for s in pt_at if pt_at[s][0] == b):
                        for tb in range(s, NT):
                            col = pt_at[s][1] + (tb - s) * P
                            ins = nc.tensor.transpose(ps[:, SC[b], col:col + P],
                                                      tmp_row(tb)[:, s * P:(s + 1) * P], ident[:])
                    ins.then_inc(pt_done, 1)

            def weigh_v(h):
                pe.wait_ge(v_ready, 2 * h + 2)
                for n, s in enumerate(pt_at):
                    b, col = pt_at[s]
                    pe.wait_ge(pt_ready, PT_BANKS * h + (b + 1))
                    for d in range(NH):
                        ins = products(ps[:, PVB[d], s * P:S], lambda part, k: v[part][:, k, d * P:(d + 1) * P],
                                       lambda part, k: pT[part][:, b * BANK + col:b * BANK + col + S - k * P],
                                       [s], first=n == 0, last=n == NT - 1)
                        if n == NT - 1:
                            ins.then_inc(pv_done, 1)

            def head(at, h, before=None):
                fresh = before is None
                if not fresh:
                    scores(before)
                    pe.wait_ge(v_taken, VV * h - 1)
                    project(at, PROJ[0]).then_inc(slab_used, 1)
                    turn_v(before)
                    project(at.plus(1), PROJ[1]).then_inc(slab_used, 1)
                    turn_p(before)
                pe.wait_ge(qk_done, QK * h + 1)
                project(at.plus(2), PROJ[0]).then_inc(slab_used, 1)
                if not fresh:
                    weigh_v(before)
                for j in range(3, PER_HEAD):
                    pe.wait_ge(qk_done, QK * h + (j - 1))
                    project(at.plus(j), PROJ[j % 2]).then_inc(slab_used, 1)

            def stay_warm(n):
                for _ in range(n):
                    ins = nc.tensor.matmul(ps[:, PROJ[0], :], warm[:, 0:P], warm, start=True, stop=True)
                ins.then_inc(warmed, 1)

            padded = [pad(0), pad(1)]

            def gate(tokens, tiles):
                return products(ps[:, GATE, tokens], lambda part, k: padded[part][:, k, :],
                                lambda part, k: hT[part][:, k, tokens], tiles, first=tiles[0] == 0,
                                last=tiles[-1] == ND - 1)

            first = At(0)
            pe.wait_ge(const_set, 1)
            stay_warm(4)
            pe.wait_ge(const_set, CONSTS)
            turn(0, 0)
            stay_warm(4)
            pe.wait_ge(warmed, 2)
            turn(0, 1)
            pe.wait_ge(hT_done, 4 * (NT // 2))
            pe.wait_ge(pad_lo, 4)
            gate(EARLY, range(0, 3 * ND // 4))
            turn(0, 2)
            gate(EARLY, range(3 * ND // 4, ND))
            project(first, PROJ[0], EARLY, range(0, ND // 2))
            turn(0, 3)
            project(first, PROJ[0], EARLY, range(ND // 2, ND))
            pe.wait_ge(hT_done, 4 * NT)
            gate(LATE, range(ND)).then_inc(f_done, 1)
            project(first, PROJ[0], LATE).then_inc(slab_used, 1)
            project(first.plus(1), PROJ[1]).then_inc(slab_used, 1)
            head(At(0, PER_HEAD, 0), 0)
            with pe.Fori(1, H) as h:
                head(At(0, PER_HEAD, h), h, before=h - 1)

            wo = At(FIRST_WO)

            def mix(cb, tb, tiles, first=False, last=False):
                at = wo.plus(2 * cb)
                return products(ps[:, YB[cb % 2][tb], :], lambda part, k: oT[part][:, k, tb * P:(tb + 1) * P],
                                lambda part, k: slab(split, at.plus(k // 4), part, k % 4, BANK),
                                tiles, first=first, last=last)

            h = H - 1
            scores(h)
            pe.wait_ge(v_taken, VV * H)
            pe.wait_ge(lo_ready, wo.count(2))
            pe.wait_ge(o_ready, NH * h)
            early, late = range(0, NH * h), range(NH * h, NK)
            mix(0, 0, early, first=True)
            mix(0, 1, early, first=True)
            turn_v(h)
            turn_p(h)
            mix(0, 2, early, first=True)
            weigh_v(h)
            mix(0, 3, early[:4], first=True).then_inc(slab_used, 1)
            mix(0, 3, early[4:])
            pe.wait_ge(o_ready, NH * H)
            for tb in range(NT):
                ins = mix(0, tb, late, last=True)
                ins.then_inc(y_done, 1)
            def half(cb, part, tb):
                pe.wait_ge(lo_ready, wo.plus(2 * cb + part).count(1))
                if part == 0 and cb >= 2:
                    pe.wait_ge(sq_done, NT + NT * (cb - 2) + tb + 1)
                ins = mix(cb, tb, range(4 * part, 4 * part + 4), first=part == 0, last=part == 1)
                if part == 1:
                    ins.then_inc(y_done, 1)
                elif tb == NT - 1:
                    ins.then_inc(slab_used, 1)

            for cb in range(1, NC - 1):
                for part in range(2):
                    for tb in range(NT):
                        half(cb, part, tb)
            for tb, part in ((0, 0), (1, 0), (0, 1), (1, 1), (2, 0), (2, 1), (3, 0), (3, 1)):
                if part == 1 and tb == 2:
                    turn(1, 0)
                half(NC - 1, part, tb)
                if part == 1 and tb == 2:
                    turn(1, 1)
            turn(1, 2)

            def ffn(g, first=False, last=False):
                at = At(FIRST_FFN, FFN, g)
                if first:
                    pe.wait_ge(hT_done, 4 * NT + 4 * (NT // 2))
                    project(at, 2, EARLY)
                    project(at.plus(1), 3, EARLY, range(0, ND // 2))
                    turn(1, 3)
                    project(at.plus(1), 3, EARLY, range(ND // 2, ND))
                    pe.wait_ge(hT_done, 4 * NT * 2)
                    project(at, 2, LATE).then_inc(slab_used, 1)
                    project(at.plus(1), 3, LATE).then_inc(slab_used, 1)
                for f in range(1 if first else 0, G):
                    if f >= 2:
                        pe.wait_ge(a_ready, G * g + (f - 1))
                    for up in range(2):
                        project(at.plus(2 * f + up), GU[f % 2][up]).then_inc(slab_used, 1)

                def down(cb, tb, tiles, start=True, stop=True):
                    a = at.plus(2 * G + cb)
                    return products(ps[:, down_bank(cb, tb, last), :],
                                    lambda part, k: oT[part][:, k, tb * P:(tb + 1) * P],
                                    lambda part, k: slab(split, a, part, k, BANK), tiles, first=start, last=stop)

                def bank_free(cb, tb):
                    before = NT * NC + nth(cb - 1, tb, last) if cb else nth(NC - 1, tb, last=False)
                    pe.wait_ge(added, (NT * NC) * g + before)

                pe.wait_ge(a_ready, G * g + (G - 1))
                pe.wait_ge(lo_ready, at.plus(2 * G).count(1))
                for tb in range(2):
                    bank_free(0, tb)
                    down(0, tb, range(G - 1), stop=False)
                pe.wait_ge(a_ready, G * g + G)
                for tb in range(2):
                    down(0, tb, [G - 1], start=False).then_inc(y_done, 1)
                for cb, tb in (LAST_DOWN if last else DOWN)[2:]:
                    pe.wait_ge(lo_ready, at.plus(2 * G + cb).count(1))
                    if not (last and cb == NC - 1):
                        bank_free(cb, tb)
                    down(cb, tb, range(G)).then_inc(y_done, 1)

            ffn(0, first=True)
            with pe.Fori(1, GROUPS - 1) as g:
                ffn(g)
            ffn(GROUPS - 1, last=True)


_INS = ["x", "norm_mix", "fox_w_in", "fox_b_f", "fox_w_out", "norm_ffn", "ffn_w_gate_up", "ffn_w_down", "final_norm"]


def kernel(**inputs):
    import numpy as _np
    import concourse.bacc as _bacc
    from concourse import mybir as _mybir
    from concourse.bass_utils import run_bass_kernel_spmd as _run

    nc = _bacc.Bacc("TRN2", target_bir_lowering=False, num_devices=1)
    arrays, args = {}, []
    for name in _INS:
        a = _np.ascontiguousarray(inputs[name])
        arrays[f"in_{name}_dram"] = a
        args.append(nc.dram_tensor(f"in_{name}_dram", a.shape, _mybir.dt.from_np(a.dtype), kind="ExternalInput").ap())
    shape = tuple(inputs["x"].shape)
    args.append(nc.dram_tensor("out_0_dram", shape, _mybir.dt.float32, kind="ExternalOutput").ap())
    fox_layer(nc, *args)
    r = _run(nc, [arrays], core_ids=[0])
    return r.results[0]["out_0_dram"]
```
